# Optimizing a Trainium2 kernel written in Bass

```python
import math
import jax, jax.numpy as jnp
from jax import lax
import numpy as np

D_MODEL = 1024
BATCH = 1
SEQ = 1024
DEPTH = 1

CHUNK = 64
POOL_WINDOWS = (2, 4, 8, 16)
N_POOL_GROUPS = len(POOL_WINDOWS)
D_POOL = D_MODEL
POOL_GROUP = D_POOL // N_POOL_GROUPS
RET_HEADS = 4
RET_DK = D_MODEL // RET_HEADS
RET_DV = 2 * D_MODEL // RET_HEADS
D_RET_QK = RET_HEADS * RET_DK
D_RET_V = RET_HEADS * RET_DV
ROPE_BASE = 10000.0
NORM_EPS = 1e-6
IN_SPLITS = (D_POOL, D_POOL, D_RET_QK, D_RET_QK, D_RET_V, D_RET_V, D_MODEL, D_MODEL)
D_IN = sum(IN_SPLITS)

kernel_name = "hybrid_pool_retention_gated_block"

def rms_norm(x, gain, eps=NORM_EPS):
    xf = x.astype(jnp.float32)
    y = xf * lax.rsqrt(jnp.mean(xf * xf, axis=-1, keepdims=True) + eps)
    return (y * gain.astype(jnp.float32)).astype(x.dtype)

def rotary(t, pos):
    half = t.shape[-1] // 2
    inv_freq = 1.0 / (ROPE_BASE ** (jnp.arange(half, dtype=jnp.float32) / half))
    ang = pos.astype(jnp.float32)[:, None] * inv_freq[None, :]
    cos = jnp.cos(ang)[None, :, None, :]
    sin = jnp.sin(ang)[None, :, None, :]
    t1, t2 = t[..., :half], t[..., half:]
    return jnp.concatenate([t1 * cos - t2 * sin, t1 * sin + t2 * cos], axis=-1)

def pool_mixer(u, w_pool, pool_scale):
    b, s, _ = u.shape
    uf = u.astype(jnp.float32)
    pos1 = jnp.arange(s, dtype=jnp.int32) + 1
    outs = []
    for g, w in enumerate(POOL_WINDOWS):
        seg = uf[..., g * POOL_GROUP:(g + 1) * POOL_GROUP]
        cs = jnp.cumsum(seg, axis=1)
        prev = jnp.pad(cs, ((0, 0), (w, 0), (0, 0)))[:, :s]
        cnt = jnp.minimum(pos1, w).astype(jnp.float32)[None, :, None]
        outs.append((cs - prev) / cnt - seg)
    pooled = jnp.stack(outs, axis=2)
    mixed = jnp.einsum('bsgc,gcd->bsgd', pooled, w_pool.astype(jnp.float32))
    mixed = mixed.reshape(b, s, D_POOL) * pool_scale.astype(jnp.float32)
    return mixed

def retention(q, k, v):
    b, s, h, dk = q.shape
    dv = v.shape[-1]
    nc = s // CHUNK
    gamma = 1.0 - jnp.exp2(-5.0 - jnp.arange(h, dtype=jnp.float32))
    log_g = jnp.log(gamma)
    idx = jnp.arange(CHUNK, dtype=jnp.float32)
    dist = jnp.abs(idx[:, None] - idx[None, :])
    decay_in = jnp.exp(log_g[:, None, None] * dist)
    xi = jnp.exp(log_g[None, :] * (idx[:, None] + 1.0))
    zeta = jnp.exp(log_g[None, :] * (CHUNK - 1.0 - idx[:, None]))
    g_chunk = jnp.exp(log_g * CHUNK)

    q = q * (dk ** -0.5)
    qc = q.reshape(b, nc, CHUNK, h, dk)
    kc = k.reshape(b, nc, CHUNK, h, dk)
    vc = v.reshape(b, nc, CHUNK, h, dv)

    scores = jnp.einsum('bnihd,bnjhd->bnhij', qc, kc) * decay_in[None, None]
    o_inner = jnp.einsum('bnhij,bnjhe->bnihe', scores, vc)

    def step(state, inp):
        q_i, k_i, v_i = inp
        cross = jnp.einsum('bihd,bhde->bihe', q_i, state) * xi[None, :, :, None]
        new_state = state * g_chunk[None, :, None, None] + jnp.einsum(
            'bihd,bihe->bhde', k_i * zeta[None, :, :, None], v_i)
        return new_state, cross

    state0 = jnp.zeros((b, h, dk, dv), jnp.float32)
    _, cross = lax.scan(step, state0, (jnp.moveaxis(qc, 1, 0), jnp.moveaxis(kc, 1, 0),
                                       jnp.moveaxis(vc, 1, 0)))
    o = o_inner + jnp.moveaxis(cross, 0, 1)
    o = o.reshape(b, s, h, dv)
    o = o * lax.rsqrt(jnp.mean(o * o, axis=-1, keepdims=True) + NORM_EPS)
    return o.reshape(b, s, h * dv)

def setup_inputs(seed: int = 0) -> dict:
    key = jax.random.key(seed)
    ks = jax.random.split(key, 10)
    f32 = jnp.float32
    x = jax.random.normal(ks[0], (BATCH, SEQ, D_MODEL), f32)
    norm_in = 1.0 + 0.02 * jax.random.normal(ks[1], (D_MODEL,), f32)
    w_in = jax.random.normal(ks[2], (D_MODEL, D_IN), f32) * D_MODEL ** -0.5
    w_pool = jax.random.normal(ks[3], (N_POOL_GROUPS, POOL_GROUP, POOL_GROUP), f32) * POOL_GROUP ** -0.5
    pool_scale = 1.0 + 0.02 * jax.random.normal(ks[4], (D_POOL,), f32)
    w_a = jax.random.normal(ks[5], (D_POOL, D_MODEL), f32) * D_POOL ** -0.5
    w_b = jax.random.normal(ks[6], (D_RET_V, D_MODEL), f32) * D_RET_V ** -0.5
    w_o = jax.random.normal(ks[7], (D_MODEL, D_MODEL), f32) * D_MODEL ** -0.5
    norm_out = 1.0 + 0.02 * jax.random.normal(ks[8], (D_MODEL,), f32)
    return {"x": x, "norm_in": norm_in, "w_in": w_in, "w_pool": w_pool,
            "pool_scale": pool_scale, "w_a": w_a, "w_b": w_b, "w_o": w_o,
            "norm_out": norm_out}

def reference(x, norm_in, w_in, w_pool, pool_scale, w_a, w_b, w_o, norm_out):
    b, s, _ = x.shape
    pos = jnp.arange(s, dtype=jnp.int32)
    for _layer in range(DEPTH):
        h = rms_norm(x, norm_in)
        proj = jnp.einsum('bsd,de->bse', h, w_in)
        offs = np.cumsum((0,) + IN_SPLITS)
        a_in, a_gate, q, k, v, r_gate, g_a, g_b = [
            proj[..., offs[i]:offs[i + 1]] for i in range(len(IN_SPLITS))]

        ya = pool_mixer(a_in, w_pool, pool_scale) * jax.nn.silu(a_gate.astype(jnp.float32))
        ya = jnp.einsum('bsc,cd->bsd', ya.astype(x.dtype), w_a)

        qf = rotary(q.astype(jnp.float32).reshape(b, s, RET_HEADS, RET_DK), pos)
        kf = rotary(k.astype(jnp.float32).reshape(b, s, RET_HEADS, RET_DK), pos)
        vf = v.astype(jnp.float32).reshape(b, s, RET_HEADS, RET_DV)
        yb = retention(qf, kf, vf) * jax.nn.silu(r_gate.astype(jnp.float32))
        yb = jnp.einsum('bsc,cd->bsd', yb.astype(x.dtype), w_b)

        merged = jax.nn.sigmoid(g_a) * ya + jax.nn.sigmoid(g_b) * yb
        x = x + jnp.einsum('bsd,de->bse', merged, w_o)
    return rms_norm(x, norm_out)


_drawn_inputs = setup_inputs


def setup_inputs(seed=0):
    import zlib

    import numpy as np

    out = dict(_drawn_inputs(seed))
    spreads = {}
    factors = {'norm_in': 3.603, 'pool_scale': 8.0, 'norm_out': 2.996}
    for name, (base, spread) in spreads.items():
        noise = np.random.default_rng([zlib.crc32(name.encode()), seed]).standard_normal(out[name].shape)
        drawn = base * np.exp(spread * noise) if base else spread * noise
        out[name] = __import__('jax').numpy.asarray(drawn.astype(out[name].dtype))
    for name, factor in factors.items():
        out[name] = (out[name] * factor).astype(out[name].dtype)
    return out
```

```python
from contextlib import ExitStack

import numpy as np
import concourse.bass as bass
from concourse import mybir

F32 = mybir.dt.float32
F32R = mybir.dt.float32r
ACT = mybir.ActivationFunctionType
ALU = mybir.AluOpType

P = 128
D_MODEL, SEQ = 1024, 1024
HALVES = 2
TOK = SEQ // HALVES
TILES = TOK // P
KT = D_MODEL // P
HEADS, DK, DV = 4, 256, 512
VT = DV // P
CHUNK = 64
WINDOWS = (2, 4, 8, 16)
GROUPS, GROUP = 4, 256
HIST = 16
EPS = 1e-6
ROPE_BASE = 10000.0
RING = 4

U_KQ = 0
U_HEAD = 4
U_V, U_G, U_F, U_WB = 0, 4, 8, 12
U_GB = U_HEAD + 16 * HEADS
U_POOL = U_GB + 4
U_MERGE = U_POOL + 4 * GROUPS
U_OUT = U_MERGE + 2 * KT
UNITS = U_OUT + 8

J_KQ = 0
J_HEAD = 4
J_G, J_F, J_WB = 0, 4, 8
J_GB = J_HEAD + 16 * HEADS
J_POOL = J_GB + 4
J_MERGE = J_POOL + 6 * GROUPS
PROJ_JOBS = J_MERGE + 2 * KT

T_HEAD = 2 * TILES
T_OT = 2 * TILES
TURN_HEAD = T_OT + VT
TURN_JOBS = T_HEAD + TURN_HEAD * HEADS

WIDE_HEAD = (3, 3, 5, 5)
WIDE_HALF = tuple(HEADS * n + 2 for n in WIDE_HEAD)

ORDER_POOL = 10 * HEADS
ORDER_HALF = ORDER_POOL + 1 + 8 * GROUPS
CONSTS = 5

HC = P + 3
PCOLS = 5 + 2 * HIST


def build(nc, wstream, x, norm_in, w_pool, pool_scale, norm_out, ident_c, trig_c, head_c, pool_c, out):
    with ExitStack() as ctx:
        def sem(name):
            return ctx.enter_context(nc.semaphore(name))

        top = [(nc.sbuf_base + 31) // 32 * 32]

        def at(name, shape, dt, offset):
            return nc.alloc_sbuf_tensor_at(name, [P, *shape], dt, offset=offset)

        def keep(name, shape, dt=F32):
            t = at(name, shape, dt, top[0])
            top[0] += (4 * int(np.prod(shape)) + 31) // 32 * 32
            return t

        hT_hi, hT_lo = keep("hT_hi", [KT, TOK], F32R), keep("hT_lo", [KT, TOK], F32R)
        w_hi, w_lo = keep("w_hi", [RING, 1024], F32R), keep("w_lo", [RING, 1024], F32R)
        w_raw = keep("w_raw", [RING, 1024])
        state_all = keep("state_all", [HEADS, 2 * DV])
        y_acc = keep("y_acc", [KT, TOK])
        ident = keep("ident", [P])
        trig = keep("trig", [2, TOK])
        head_k = keep("head_k", [HEADS, HC])
        pool_k = keep("pool_k", [HALVES * GROUPS, PCOLS])
        history = keep("history", [GROUPS, 2 * HIST])
        gain_in = keep("gain_in", [KT])
        scale_k = keep("scale_k", [KT])
        ssq, ms, rstd, minus_half, eps_k, eps_head, zeta, inv_dv, inv_dm = (keep(n, [1]) for n in (
            "ssq", "ms", "rstd", "minus_half", "eps_k", "eps_head", "zeta", "inv_dv", "inv_dm"))
        tab_tmp = keep("tab_tmp", [2 * HIST])

        R, K = top[0], 1024
        v_hi, v_lo = at("v_hi", [TILES, DV], F32R, R), at("v_lo", [TILES, DV], F32R, R + 8 * K)
        yb_hi, yb_lo = at("yb_hi", [VT, TOK], F32R, R + 16 * K), at("yb_lo", [VT, TOK], F32R, R + 24 * K)
        kq = at("kq", [4, TOK], F32, R + 32 * K)
        gate = at("gate", [VT, TOK], F32, R + 40 * K)
        o_n = at("o_n", [TILES, DV], F32, R + 48 * K)
        st_hi, st_lo = at("st_hi", [2, DV], F32R, R + 56 * K), at("st_lo", [2, DV], F32R, R + 60 * K)
        state = at("state", [2, DV], F32, R + 64 * K)
        rope_in = at("rope_in", [2, TOK], F32, R + 68 * K)
        pair = at("pair", [2, TOK], F32, R + 72 * K)
        sig = at("sig", [TOK], F32, R + 76 * K)
        junk = at("junk", [DV], F32, R + 78 * K)
        sc_f, sc_hi, sc_lo = (at(n, [P], d, R + 80 * K + i * 512) for i, (n, d) in enumerate(
            (("sc_f", F32), ("sc_hi", F32R), ("sc_lo", F32R))))
        kn_f, kn_hi, kn_lo, q_hi, q_lo = (at(n, [DK], d, R + 81 * K + 512 + i * K) for i, (n, d) in enumerate(
            (("kn_f", F32), ("kn_hi", F32R), ("kn_lo", F32R), ("q_hi", F32R), ("q_lo", F32R))))
        h_f = at("h_f", [2, TOK], F32, R + 32 * K)
        h_junk = at("h_junk", [D_MODEL], F32, R + 40 * K)
        ya_hi, ya_lo = at("ya_hi", [KT, TOK], F32R, R), at("ya_lo", [KT, TOK], F32R, R + 16 * K)
        row = HIST + TOK
        a_in, pa, pb = (at(n, [2, row], F32, R + 32 * K + i * 8 * row) for i, n in enumerate(("a_in", "pa", "pb")))
        po_f, po_hi, po_lo = (at(n, [2, TOK], d, R + 45 * K + 4 * K * i) for i, (n, d) in enumerate(
            (("po_f", F32), ("po_hi", F32R), ("po_lo", F32R))))
        wp_hi, wp_lo = at("wp_hi", [2 * GROUP], F32R, R + 57 * K), at("wp_lo", [2 * GROUP], F32R, R + 59 * K)
        wp_raw = at("wp_raw", [GROUPS, 2 * GROUP], F32, R + 64 * K)
        a_sig, a_gate, ya_f = (at(n, [2, TOK], F32, R + (72 + 4 * i) * K) for i, n in enumerate(
            ("a_sig", "a_gate", "ya_f")))
        m_hi, m_lo = at("m_hi", [KT, TOK], F32R, R + 32 * K), at("m_lo", [KT, TOK], F32R, R + 48 * K)
        x_sb = at("x_sb", [TILES, D_MODEL], F32, R + 64 * K)
        gain_out = at("gain_out", [D_MODEL], F32, R + 80 * K)
        m_sig = at("m_sig", [TOK], F32, R + 84 * K)
        m_f, m_a = trig[:, 0, :], trig[:, 1, :]
        out_junk = at("out_junk", [D_MODEL], F32, R)
        assert R + 86 * K + 512 <= nc.sbuf_usable_end, R

        proj = [ctx.enter_context(nc.psum_tensor(f"proj{i}", [P, 512], F32)) for i in range(2)]
        wide = [ctx.enter_context(nc.psum_tensor(f"wide{i}", [P, 512], F32)) for i in range(4)]
        turn = [ctx.enter_context(nc.psum_tensor(f"turn{i}", [P, 512], F32)) for i in range(2)]

        consts_in = sem("consts_in")
        raw_in = [sem(f"raw_in{i}") for i in range(RING)]
        x_in = [sem(f"x_in{i}") for i in range(TILES)]
        trig_in, wp_in, gain_out_in = sem("trig_in"), sem("wp_in"), sem("gain_out_in")
        stored = [sem(f"stored{i}") for i in range(TILES)]
        unit_done = sem("unit_done")
        wb_first = sem("wb_first")
        mix_done = sem("mix_done")
        turn_full = sem("turn_full")
        o_full, upd_full = sem("o_full"), sem("upd_full")
        proj_free = [sem(f"proj_free{i}") for i in range(2)]
        turn_free = [sem(f"turn_free{i}") for i in range(2)]
        wide_free = [sem(f"wide_free{i}") for i in range(4)]
        w_hi_s, w_lo_s = sem("w_hi_ready"), sem("w_lo_ready")
        h_hi_s, h_lo_s = sem("h_hi_ready"), sem("h_lo_ready")
        v_hi_s, q_hi_s, q_lo_s = sem("v_hi_ready"), sem("q_hi_ready"), sem("q_lo_ready")
        sc_hi_s, sc_lo_s = sem("sc_hi_ready"), sem("sc_lo_ready")
        kn_hi_s, kn_lo_s = sem("kn_hi_ready"), sem("kn_lo_ready")
        st_hi_s, st_lo_s = sem("st_hi_ready"), sem("st_lo_ready")
        yb_hi_s, yb_lo_s = sem("yb_hi_ready"), sem("yb_lo_ready")
        po_hi_s, po_lo_s = sem("po_hi_ready"), sem("po_lo_ready")
        wp_hi_s, wp_lo_s = sem("wp_hi_ready"), sem("wp_lo_ready")
        ya_hi_s, ya_lo_s = sem("ya_hi_ready"), sem("ya_lo_ready")
        m_hi_s, m_lo_s = sem("m_hi_ready"), sem("m_lo_ready")
        x_sq, x_rstd, x_scaled = sem("x_sq"), sem("x_rstd"), sem("x_scaled")
        o_sq, o_rstd = sem("o_sq"), sem("o_rstd")
        y_sq, y_rstd, y_ready = sem("y_sq"), sem("y_rstd"), sem("y_ready")
        rope_done = sem("rope_done")
        gate_sig, sig_used, a_sig_s = sem("gate_sig"), sem("sig_used"), sem("a_sig_ready")
        pooled = sem("pooled")
        m_sum = sem("m_sum")
        acc_zero = sem("acc_zero")
        dve_order, pool_order = sem("dve_order"), sem("pool_order")
        zeroed = sem("zeroed")
        zeta_ready = sem("zeta_ready")
        merged = sem("merged")

        x_t = x.rearrange("b (h t p) d -> (b h) t p d", h=HALVES, t=TILES)
        out_t = out.rearrange("b (h t p) d -> (b h) t p d", h=HALVES, t=TILES)

        block = ctx.enter_context(nc.Block())

        class Place:

            def __init__(self, half, s=0, units=0, projs=0):
                self.half, self.s, self.units, self.projs = half, s, units, projs

            def split(self, u):
                return self.half * UNITS + self.s * self.units + (u + 1)

            def used(self, u):
                return self.half * UNITS + self.s * self.units + (u + 2)

            def loaded(self, u):
                return self.half * (16 * UNITS // RING) + self.s * (16 * self.units // RING) + 16 * (u // RING + 1)

            def proj_open(self, j):
                return self.half * (PROJ_JOBS // 2) + self.s * (self.projs // 2) + (j // 2 + 1)

            def proj_read(self, j):
                return self.proj_open(j) + 1

            def turn_open(self, j):
                return self.half * (TURN_JOBS // 2) + self.s * (TURN_HEAD // 2) + (j // 2 + 1)

            def turn_read(self, j):
                return self.turn_open(j) + 1

            def turned(self, j):
                return self.half * TURN_JOBS + self.s * TURN_HEAD + (j + 1)

            def wide_open(self, b, n):
                return self.half * WIDE_HALF[b] + self.s * WIDE_HEAD[b] + (n + 1)

            def nth(self, n, per_step, per_half):
                return self.half * per_half + self.s * per_step + n

        def at_head(half, h):
            return Place(half, h, 16, 16)

        def at_group(half, g):
            return Place(half, g, 4, 6)

        def at_merge(half, i):
            return Place(half, i, 4, 4)

        def at_out(half, e):
            return Place(half, e, 4, 0)

        @block.sync
        def _(sp):
            for t in range(TILES):
                sp.dma_start(x_sb[:, t, :], x_t[0, t]).then_inc(x_in[t], 16)
            sp.dma_start(ident[:], ident_c).then_inc(consts_in, 16)
            sp.dma_start(gain_in[:], norm_in).then_inc(consts_in, 16)
            for r in range(RING):
                sp.dma_start(w_raw[:, r, :], wstream[r]).then_inc(raw_in[r], 16)
            sp.dma_start(trig[:], trig_c[0]).then_inc(trig_in, 16)
            sp.dma_start(head_k[:], head_c).then_inc(consts_in, 16)
            sp.dma_start(pool_k[:], pool_c).then_inc(consts_in, 16)
            sp.dma_start(scale_k[:], pool_scale).then_inc(consts_in, 16)

            def load_units(half, first, last):
                with sp.Fori(first // RING, last // RING) as q:
                    for r in range(RING):
                        sp.wait_ge(w_lo_s, half * UNITS + q * RING + (r + 1))
                        sp.dma_start(w_raw[:, r, :], wstream[q * RING + (RING + r)]).then_inc(raw_in[r], 16)

            with sp.Fori(0, HALVES) as half:
                here = Place(half)
                load_units(half, 0, U_POOL)
                sp.wait_ge(sig_used, here.nth(4, 0, 4))
                sp.dma_start(wp_raw[:], w_pool).then_inc(wp_in, 16)
                load_units(half, U_POOL, U_MERGE)
                sp.wait_ge(ya_lo_s, here.nth(KT, 0, KT))
                for t in range(TILES):
                    sp.dma_start(x_sb[:, t, :], x_t[half, t]).then_inc(x_in[t], 16)
                sp.dma_start(gain_out[:], norm_out).then_inc(gain_out_in, 16)
                load_units(half, U_MERGE, UNITS - RING)
                for r in range(RING):
                    sp.wait_ge(w_lo_s, here.split(UNITS - RING + r))
                    sp.dma_start(w_raw[:, r, :], wstream[r]).then_inc(raw_in[r], 16)
                for t in range(TILES):
                    sp.wait_ge(y_ready, here.nth(t + 1, 0, TILES))
                    sp.dma_start(out_t[half, t], x_sb[:, t, :]).then_inc(stored[t], 16)
                for t in range(TILES):
                    sp.wait_ge(stored[t], here.nth(16, 0, 16))
                    sp.dma_start(x_sb[:, t, :], x_t[HALVES - 1, t]).then_inc(x_in[t], 16)
                sp.wait_ge(m_lo_s, here.nth(KT, 0, KT))
                sp.dma_start(trig[:], trig_c[HALVES - 1]).then_inc(trig_in, 16)
            for t in range(TILES):
                sp.wait_ge(x_in[t], 16 * (2 * HALVES + 1))
            sp.wait_ge(trig_in, 16 * (HALVES + 1))
            for r in range(RING):
                sp.wait_ge(raw_in[r], 16 * (HALVES * UNITS // RING + 1))

        @block.tensor
        def _(pe):
            def mm3(dst, a_hi, a_lo, b_hi, b_lo, first, last):
                nc.tensor.matmul(dst, a_hi, b_hi, start=first, stop=False)
                nc.tensor.matmul(dst, a_hi, b_lo, start=False, stop=False)
                return nc.tensor.matmul(dst, a_lo, b_hi, start=False, stop=last)

            def slot(u, k):
                s = u % RING
                return (w_hi[:, s, :].rearrange("p (k e) -> p k e", k=k),
                        w_lo[:, s, :].rearrange("p (k e) -> p k e", k=k))

            def project(here, u, j, b_hi, b_lo):
                pe.wait_ge(w_lo_s, here.split(u))
                pe.wait_ge(proj_free[j % 2], here.proj_open(j))
                wh, wl = slot(u, KT)
                for k in range(KT):
                    mm = mm3(proj[j % 2][:], wh[:, k, :], wl[:, k, :], b_hi[:, k, :], b_lo[:, k, :],
                             k == 0, k == KT - 1)
                mm.then_inc(unit_done, 1)

            def natural(here, u, n, a_hi, a_lo):
                pe.wait_ge(w_lo_s, here.split(u))
                wh, wl = slot(u, 2)
                for t in range(TILES):
                    cols = slice(t * P, (t + 1) * P)
                    for k in range(2):
                        mm = mm3(wide[t][:], a_hi[:, 2 * n + k, cols], a_lo[:, 2 * n + k, cols],
                                 wh[:, k, :], wl[:, k, :], n == 0 and k == 0, n == 3 and k == 1)
                mm.then_inc(unit_done, 1)

            def head(half, h):
                here = at_head(half, h)
                for b in range(4):
                    pe.wait_ge(wide_free[b], here.wide_open(b, 0))
                for u in range(4):
                    natural(here, U_HEAD + U_V + u, u, hT_hi, hT_lo)
                pe.wait_ge(rope_done, here.nth(3, 2, 2 * HEADS))
                for t in range(TILES):
                    cols = slice(t * P, (t + 1) * P)
                    pe.wait_ge(turn_free[0], here.turn_open(T_HEAD + 2 * t))
                    for j in range(2):
                        mm = nc.tensor.matmul(turn[0][:, 0:P], kq[:, j, cols], kq[:, 2 + j, cols],
                                              start=j == 0, stop=j == 1)
                    mm.then_inc(turn_full, 1)
                    pe.wait_ge(turn_free[1], here.turn_open(T_HEAD + 2 * t + 1))
                    for j in range(2):
                        mm = nc.tensor.transpose(turn[1][:, j * P:(j + 1) * P], kq[:, j, cols], ident[:])
                    mm.then_inc(turn_full, 1)
                    project(here, U_HEAD + U_G + t, J_HEAD + J_G + t, hT_hi, hT_lo)
                    o = wide[t % 2]
                    pe.wait_ge(wide_free[t % 2], here.wide_open(t % 2, 1 + t // 2))
                    pe.wait_ge(sc_lo_s, here.nth(t + 1, 4, 16))
                    mm3(o[:], sc_hi[:], sc_lo[:], v_hi[:, t, :], v_lo[:, t, :], True, False)
                    pe.wait_ge(q_lo_s, here.nth(t + 1, 4, 16))
                    pe.wait_ge(st_lo_s, here.nth(t + 1, 4, 16))
                    for j in range(2):
                        mm = mm3(o[:], q_hi[:, j * P:(j + 1) * P], q_lo[:, j * P:(j + 1) * P],
                                 st_hi[:, j, :], st_lo[:, j, :], False, j == 1)
                    mm.then_inc(o_full, 1)
                    pe.wait_ge(kn_lo_s, here.nth(t + 1, 4, 16))
                    for j in range(2):
                        pe.wait_ge(wide_free[2 + j], here.wide_open(2 + j, 1 + t))
                        mm = mm3(wide[2 + j][:], kn_hi[:, j * P:(j + 1) * P], kn_lo[:, j * P:(j + 1) * P],
                                 v_hi[:, t, :], v_lo[:, t, :], True, True)
                    mm.then_inc(upd_full, 1)

                def filler(i):
                    project(here, U_HEAD + U_F + i, J_HEAD + J_F + i, hT_hi, hT_lo)

                def turn_o(c):
                    pe.wait_ge(turn_free[c % 2], here.turn_open(T_HEAD + T_OT + c))
                    for t in range(TILES):
                        mm = nc.tensor.transpose(turn[c % 2][:, t * P:(t + 1) * P],
                                                 o_n[:, t, c * P:(c + 1) * P], ident[:])
                    mm.then_inc(turn_full, 1)

                filler(0)
                for b in range(2):
                    pe.wait_ge(wide_free[b], here.wide_open(b, 3))
                turn_o(0)
                turn_o(1)
                filler(1)
                turn_o(2)
                turn_o(3)
                filler(2)
                filler(3)
                pe.wait_ge(yb_lo_s, here.nth(VT, VT, HEADS * VT))
                for i in range(4):
                    u = U_HEAD + U_WB + i
                    pe.wait_ge(w_lo_s, here.split(u))
                    wh, wl = slot(u, VT)
                    for d in range(2):
                        pe.wait_ge(proj_free[d], here.proj_open(J_HEAD + J_WB + 2 * i + d))
                        for k in range(VT):
                            mm = mm3(proj[d][:], wh[:, k, d * P:(d + 1) * P], wl[:, k, d * P:(d + 1) * P],
                                     yb_hi[:, k, :], yb_lo[:, k, :], k == 0, k == VT - 1)
                        mm.then_inc(unit_done if d else wb_first, 1)

            pe.sem_inc(unit_done, 1)
            pe.wait_ge(consts_in, 16 * CONSTS)
            with pe.Fori(0, HALVES) as half:
                here = Place(half)
                for t in range(TILES):
                    pe.wait_ge(x_scaled, here.nth(t + 1, 0, TILES))
                    for r in range(2):
                        pe.wait_ge(turn_free[r], here.turn_open(2 * t + r))
                        for k in range(4):
                            d = (4 * r + k) * P
                            mm = nc.tensor.transpose(turn[r][:, k * P:(k + 1) * P], x_sb[:, t, d:d + P], ident[:])
                        mm.then_inc(turn_full, 1)
                pe.wait_ge(h_lo_s, here.nth(2 * TILES, 0, 2 * TILES))
                for i in range(4):
                    project(here, U_KQ + i, J_KQ + i, hT_hi, hT_lo)
                with pe.Fori(0, HEADS - 1) as h:
                    head(half, h)
                head(half, HEADS - 1)
                for i in range(4):
                    project(here, U_GB + i, J_GB + i, hT_hi, hT_lo)
                with pe.Fori(0, GROUPS) as g:
                    here = at_group(half, g)
                    for i in range(4):
                        project(here, U_POOL + i, J_POOL + i, hT_hi, hT_lo)
                    pe.wait_ge(wp_lo_s, here.nth(1, 1, GROUPS))
                    pe.wait_ge(po_lo_s, here.nth(1, 1, GROUPS))
                    for j in range(2):
                        pe.wait_ge(proj_free[j], here.proj_open(J_POOL + 4 + j))
                        for k in range(2):
                            e = k * GROUP + j * P
                            mm = mm3(proj[j][:], wp_hi[:, e:e + P], wp_lo[:, e:e + P],
                                     po_hi[:, k, :], po_lo[:, k, :], k == 0, k == 1)
                        mm.then_inc(mix_done, 1)
                with pe.Fori(0, KT // 2) as i:
                    here = at_merge(half, i)
                    pe.wait_ge(ya_lo_s, Place(half).nth(KT, 0, KT))
                    for d in range(2):
                        project(here, U_MERGE + 2 * d, J_MERGE + 2 * d, ya_hi, ya_lo)
                        project(here, U_MERGE + 2 * d + 1, J_MERGE + 2 * d + 1, hT_hi, hT_lo)
                with pe.Fori(0, 2) as e:
                    here = at_out(half, e)
                    pe.wait_ge(m_lo_s, Place(half).nth(KT, 0, KT))
                    for b in range(4):
                        pe.wait_ge(wide_free[b], half * WIDE_HALF[b] + e + (WIDE_HALF[b] - 1))
                    for u in range(4):
                        natural(here, U_OUT + u, u, m_hi, m_lo)

        @block.scalar
        def _(act):
            def copy(dst, src):
                return nc.scalar.activation(dst, src, ACT.Copy)

            def split_w(here, u):
                s = (u + 3) % RING
                act.wait_ge(raw_in[s], here.loaded(u + 3))
                act.wait_ge(unit_done, here.used(u - 1))
                copy(w_hi[:, s, :], w_raw[:, s, :]).then_inc(w_hi_s, 1)

            def rope_copy(here, u, j, rope):
                act.wait_ge(unit_done, here.used(u))
                if j % 2 == 0:
                    act.wait_ge(rope_done, rope)
                copy(rope_in[:, j % 2, :], proj[j % 2][:]).then_inc(proj_free[j % 2], 1)

            def head(half, h, closing):
                here = at_head(half, h)
                copy(zeta[:], head_k[:, h, P:P + 1]).then_inc(zeta_ready, 1)
                for u in range(4):
                    split_w(here, U_HEAD + U_V + u)
                act.wait_ge(unit_done, here.used(U_HEAD + U_V + 3))
                copy(st_hi[:].rearrange("p j e -> p (j e)"), state_all[:, h, :]).then_inc(st_hi_s, 1)
                for t in range(TILES):
                    copy(v_hi[:, t, :], wide[t][:]).then_inc(v_hi_s, 1)
                act.wait_ge(zeta_ready, here.nth(1, 1, HEADS))
                act.wait_ge(rope_done, here.nth(3, 2, 2 * HEADS))
                for t in range(TILES):
                    cols = slice(t * P, (t + 1) * P)
                    if t:
                        act.wait_ge(o_full, here.nth(t, 4, 16))
                        act.wait_ge(q_lo_s, here.nth(t, 4, 16))
                    copy(q_hi[:].rearrange("p (j s) -> p j s", j=2), kq[:, 2:4, cols]).then_inc(q_hi_s, 1)
                    act.wait_ge(turn_free[0], here.turn_read(T_HEAD + 2 * t))
                    copy(sc_hi[:], sc_f[:]).then_inc(sc_hi_s, 1)
                    act.wait_ge(turn_full, here.turned(T_HEAD + 2 * t + 1))
                    if t:
                        act.wait_ge(upd_full, here.nth(t, 4, 16))
                        act.wait_ge(kn_lo_s, here.nth(t, 4, 16))
                    nc.scalar.activation(kn_f[:], turn[1][:, 0:DK], ACT.Copy,
                                         scale=zeta[:]).then_inc(turn_free[1], 1)
                    act.wait_ge(turn_free[1], here.turn_read(T_HEAD + 2 * t + 1))
                    copy(kn_hi[:], kn_f[:]).then_inc(kn_hi_s, 1)
                    split_w(here, U_HEAD + U_G + t)
                    act.wait_ge(unit_done, here.used(U_HEAD + U_G + t))
                    if t:
                        act.wait_ge(proj_free[(t - 1) % 2], here.proj_read(J_HEAD + J_G + t - 1))
                    nc.scalar.activation(sig[:], proj[t % 2][:], ACT.Sigmoid).then_inc(gate_sig, 1)
                    act.wait_ge(o_full, here.nth(t + 1, 4, 16))
                    nc.scalar.activation(junk[:], wide[t % 2][:], ACT.Square, accum_out=ssq[:]).then_inc(o_sq, 1)
                    if t < TILES - 1:
                        for j in range(2):
                            act.wait_ge(wide_free[2 + j], here.wide_open(2 + j, 2 + t))
                        copy(st_hi[:], state[:]).then_inc(st_hi_s, 1)
                    act.wait_ge(o_rstd, here.nth(t + 1, 4, 16))
                    nc.scalar.activation(o_n[:, t, :], wide[t % 2][:], ACT.Copy,
                                         scale=rstd[:]).then_inc(wide_free[t % 2], 1)

                def filled(i):
                    u, j = U_HEAD + U_F + i, J_HEAD + J_F + i
                    if closing:
                        act.wait_ge(unit_done, here.used(u))
                        nc.scalar.activation(kq[:, i, :], proj[i % 2][:], ACT.Sigmoid).then_inc(proj_free[i % 2], 1)
                    else:
                        rope_copy(here, u, j, here.nth(3 + i // 2, 2, 2 * HEADS))

                def split_yb(c):
                    act.wait_ge(turn_free[c % 2], here.turn_read(T_HEAD + T_OT + c))
                    copy(yb_hi[:, c, :], pair[:, c % 2, :]).then_inc(yb_hi_s, 1)

                split_w(here, U_HEAD + U_F)
                filled(0)
                split_yb(0)
                split_yb(1)
                split_w(here, U_HEAD + U_F + 1)
                filled(1)
                split_yb(2)
                split_yb(3)
                for i in (2, 3):
                    split_w(here, U_HEAD + U_F + i)
                    filled(i)
                for i in range(4):
                    split_w(here, U_HEAD + U_WB + i)

            for u in range(RING - 1):
                act.wait_ge(raw_in[u], 16)
                copy(w_hi[:, u, :], w_raw[:, u, :]).then_inc(w_hi_s, 1)
            act.wait_ge(consts_in, 16 * CONSTS)
            with act.Fori(0, HALVES) as half:
                here = Place(half)

                def split_h(t, r):
                    act.wait_ge(turn_free[r], here.turn_read(2 * t + r))
                    copy(hT_hi[:, 4 * r:4 * r + 4, t * P:(t + 1) * P],
                         h_f[:, r, :].rearrange("p (k s) -> p k s", k=4)).then_inc(h_hi_s, 1)

                for t in range(TILES):
                    act.wait_ge(x_in[t], half * 32 + 16)
                    nc.scalar.activation(h_junk[:], x_sb[:, t, :], ACT.Square, accum_out=ssq[:]).then_inc(x_sq, 1)
                    act.wait_ge(x_rstd, here.nth(t + 1, 0, TILES))
                    nc.scalar.activation(x_sb[:, t, :], x_sb[:, t, :], ACT.Copy, scale=rstd[:]).then_inc(x_scaled, 1)
                    if t:
                        split_h(t - 1, 0)
                        split_h(t - 1, 1)
                split_h(TILES - 1, 0)
                split_h(TILES - 1, 1)
                for i in range(4):
                    split_w(here, U_KQ + i)
                    rope_copy(here, U_KQ + i, J_KQ + i, here.nth(1 + i // 2, 2, 2 * HEADS))
                with act.Fori(0, HEADS - 1) as h:
                    head(half, h, False)
                head(half, HEADS - 1, True)
                for i in range(4):
                    split_w(here, U_GB + i)
                    act.wait_ge(unit_done, here.used(U_GB + i))
                    if i:
                        act.wait_ge(sig_used, here.nth(i, 0, 4))
                    nc.scalar.activation(sig[:], proj[i % 2][:], ACT.Sigmoid).then_inc(proj_free[i % 2], 1)
                with act.Fori(0, GROUPS) as g:
                    here = at_group(half, g)
                    for i in range(2):
                        split_w(here, U_POOL + i)
                        act.wait_ge(unit_done, here.used(U_POOL + i))
                        if i == 0:
                            act.wait_ge(pooled, here.nth(1, 1, GROUPS))
                        copy(a_in[:, i, HIST:], proj[i][:]).then_inc(proj_free[i], 1)
                    act.wait_ge(wp_in, half * 16 + 16)
                    copy(wp_hi[:], wp_raw[:, g, :]).then_inc(wp_hi_s, 1)
                    for i in range(2):
                        split_w(here, U_POOL + 2 + i)
                        act.wait_ge(unit_done, here.used(U_POOL + 2 + i))
                        nc.scalar.activation(a_sig[:, i, :], proj[i][:], ACT.Sigmoid).then_inc(a_sig_s, 1)
                        if i == 0:
                            act.wait_ge(pooled, here.nth(2, 1, GROUPS))
                            copy(po_hi[:], po_f[:]).then_inc(po_hi_s, 1)
                    for j in range(2):
                        act.wait_ge(proj_free[j], here.proj_read(J_POOL + 4 + j))
                        copy(ya_hi[:, g * 2 + j, :], ya_f[:, j, :]).then_inc(ya_hi_s, 1)
                with act.Fori(0, KT // 2) as i:
                    here = at_merge(half, i)
                    for d in range(2):
                        for n in range(2):
                            split_w(here, U_MERGE + 2 * d + n)
                        act.wait_ge(unit_done, here.used(U_MERGE + 2 * d + 1))
                        nc.scalar.activation(m_sig[:], proj[1][:], ACT.Sigmoid).then_inc(proj_free[1], 1)
                        act.wait_ge(m_sum, here.nth(d + 1, 2, KT))
                        copy(m_hi[:, i * 2 + d, :], m_f).then_inc(m_hi_s, 1)
                with act.Fori(0, 2) as e:
                    here = at_out(half, e)
                    for u in range(4):
                        split_w(here, U_OUT + u)
                here = Place(half)
                for t in range(TILES):
                    act.wait_ge(wide_free[t], half * WIDE_HALF[t] + (WIDE_HALF[t] + 1))
                    nc.scalar.activation(out_junk[:], x_sb[:, t, :], ACT.Square, accum_out=ssq[:]).then_inc(y_sq, 1)
                    act.wait_ge(y_rstd, here.nth(t + 1, 0, TILES))

        @block.gpsimd
        def _(pool):
            count = [0]

            def link(ins, base):
                count[0] += 1
                ins.then_inc(pool_order, 1)
                pool.wait_ge(pool_order, base + count[0])

            def rms(base, inv_n, eps):
                count[0] = 0
                link(nc.gpsimd.tensor_tensor(ms[:], ssq[:], inv_n[:], ALU.mult), base)
                link(nc.gpsimd.tensor_tensor(ms[:], ms[:], eps[:], ALU.add), base)
                return nc.gpsimd.tensor_tensor(rstd[:], ms[:], minus_half[:], ALU.pow)

            for t, value in ((minus_half, -0.5), (eps_k, EPS), (inv_dv, 1.0 / DV), (inv_dm, 1.0 / D_MODEL)):
                nc.gpsimd.memset(t[:], value).then_inc(pool_order, 1)
            nc.gpsimd.memset(y_acc[:], 0.0).then_inc(acc_zero, 1)
            pool.wait_ge(pool_order, 4)
            pool.wait_ge(consts_in, 16 * CONSTS)
            pool.sem_inc(merged, 1)
            x_part, head_part = 2 * TILES, 2 * TILES + 1
            with pool.Fori(0, HALVES) as half:
                here = Place(half)
                order = half * (2 * x_part + HEADS * head_part) + 4
                for t in range(TILES):
                    pool.wait_ge(x_sq, here.nth(t + 1, 0, TILES))
                    rms(order + 2 * t, inv_dm, eps_k).then_inc(x_rstd, 1)
                with pool.Fori(0, HEADS) as h:
                    nc.gpsimd.tensor_copy(eps_head[:], head_k[:, h, P + 1:P + 2]).then_inc(pool_order, 1)
                    pool.wait_ge(pool_order, order + h * head_part + (x_part + 1))
                    for t in range(TILES):
                        pool.wait_ge(o_sq, at_head(half, h).nth(t + 1, 4, 16))
                        rms(order + h * head_part + (x_part + 1 + 2 * t), inv_dv, eps_head).then_inc(o_rstd, 1)
                pool.wait_ge(m_sum, here.nth(KT, 0, KT))
                pool.sem_inc(merged, 1)
                nc.gpsimd.memset(y_acc[:], 0.0).then_inc(acc_zero, 1)
                for t in range(TILES):
                    pool.wait_ge(y_sq, here.nth(t + 1, 0, TILES))
                    if t:
                        pool.wait_ge(y_ready, here.nth(t, 0, TILES))
                    rms(order + HEADS * head_part + (x_part + 2 * t), inv_dm, eps_k).then_inc(y_rstd, 1)

        @block.vector
        def _(dve):
            def rest(dst, src, hi):
                return nc.vector.tensor_tensor(dst, src, hi.bitcast(F32), ALU.subtract)

            def split_w(here, u):
                s = (u + 3) % RING
                dve.wait_ge(w_hi_s, here.split(u + 3))
                rest(w_lo[:, s, :], w_raw[:, s, :], w_hi[:, s, :]).then_inc(w_lo_s, 1)

            def rotate(here, j, order, done, n):
                for i in range(2):
                    dve.wait_ge(proj_free[i], here.proj_read(j - 1 + i))
                dve.wait_ge(rope_done, done)
                t1, t2 = rope_in[:, 0, :], rope_in[:, 1, :]
                cos, sin = trig[:, 0, :], trig[:, 1, :]
                for i, (first, second, op) in enumerate(((cos, sin, ALU.subtract), (sin, cos, ALU.add))):
                    nc.vector.tensor_tensor(pair[:, 0, :], t1, first, ALU.mult).then_inc(dve_order, 1)
                    nc.vector.tensor_tensor(pair[:, 1, :], t2, second, ALU.mult).then_inc(dve_order, 1)
                    dve.wait_ge(dve_order, order + 3 * i + 2)
                    ins = nc.vector.tensor_tensor(kq[:, n + i, :], pair[:, 0, :], pair[:, 1, :], op)
                    ins.then_inc(rope_done if i else dve_order, 1)
                    if i == 0:
                        dve.wait_ge(dve_order, order + 3)

            def head(half, h, closing):
                here = at_head(half, h)
                for u in range(4):
                    split_w(here, U_HEAD + U_V + u)
                dve.wait_ge(st_hi_s, here.nth(1, 4, 16))
                rest(st_lo[:].rearrange("p j e -> p (j e)"), state_all[:, h, :],
                     st_hi[:].rearrange("p j e -> p (j e)")).then_inc(st_lo_s, 1)
                for t in range(TILES):
                    dve.wait_ge(v_hi_s, here.nth(t + 1, 4, 16))
                    rest(v_lo[:, t, :], wide[t][:], v_hi[:, t, :]).then_inc(wide_free[t], 1)
                for t in range(TILES):
                    cols = slice(t * P, (t + 1) * P)
                    dve.wait_ge(turn_full, here.turned(T_HEAD + 2 * t))
                    nc.vector.tensor_tensor(sc_f[:], turn[0][:, 0:P], head_k[:, h, 0:P], ALU.mult)\
                        .then_inc(turn_free[0], 1)
                    dve.wait_ge(q_hi_s, here.nth(t + 1, 4, 16))
                    rest(q_lo[:].rearrange("p (j s) -> p j s", j=2), kq[:, 2:4, cols],
                         q_hi[:].rearrange("p (j s) -> p j s", j=2)).then_inc(q_lo_s, 1)
                    dve.wait_ge(sc_hi_s, here.nth(t + 1, 4, 16))
                    rest(sc_lo[:], sc_f[:], sc_hi[:]).then_inc(sc_lo_s, 1)
                    dve.wait_ge(kn_hi_s, here.nth(t + 1, 4, 16))
                    rest(kn_lo[:], kn_f[:], kn_hi[:]).then_inc(kn_lo_s, 1)
                    split_w(here, U_HEAD + U_G + t)
                    dve.wait_ge(gate_sig, here.nth(t + 1, 4, 16))
                    nc.vector.tensor_tensor(gate[:, t, :], proj[t % 2][:], sig[:], ALU.mult)\
                        .then_inc(proj_free[t % 2], 1)
                    dve.wait_ge(upd_full, here.nth(t + 1, 4, 16))
                    for j in range(2):
                        kept = state_all[:, h, j * DV:(j + 1) * DV]
                        nc.vector.scalar_tensor_tensor(
                            out=kept if t == TILES - 1 else state[:, j, :], in0=kept if t == 0 else state[:, j, :],
                            scalar=head_k[:, h, P + 2:P + 3], in1=wide[2 + j][:], op0=ALU.mult, op1=ALU.add)\
                            .then_inc(wide_free[2 + j], 1)
                    if t < TILES - 1:
                        dve.wait_ge(st_hi_s, here.nth(t + 2, 4, 16))
                        rest(st_lo[:], state[:], st_hi[:]).then_inc(st_lo_s, 1)

                def gate_o(c):
                    dve.wait_ge(turn_full, here.turned(T_HEAD + T_OT + c))
                    if c >= 2:
                        dve.wait_ge(yb_lo_s, here.nth(c - 1, 4, 16))
                    nc.vector.tensor_tensor(pair[:, c % 2, :], turn[c % 2][:], gate[:, c, :], ALU.mult)\
                        .then_inc(turn_free[c % 2], 1)

                def split_yb(c):
                    dve.wait_ge(yb_hi_s, here.nth(c + 1, 4, 16))
                    rest(yb_lo[:, c, :], pair[:, c % 2, :], yb_hi[:, c, :]).then_inc(yb_lo_s, 1)

                split_w(here, U_HEAD + U_F)
                gate_o(0)
                gate_o(1)
                split_yb(0)
                split_yb(1)
                split_w(here, U_HEAD + U_F + 1)
                gate_o(2)
                gate_o(3)
                split_yb(2)
                split_yb(3)
                order = half * ORDER_HALF + h * 10 + 10
                if not closing:
                    dve.wait_ge(yb_lo_s, here.nth(VT, 4, 16))
                    rotate(here, J_HEAD + J_F + 1, order, here.nth(3, 2, 2 * HEADS), 0)
                split_w(here, U_HEAD + U_F + 2)
                split_w(here, U_HEAD + U_F + 3)
                if not closing:
                    rotate(here, J_HEAD + J_F + 3, order + 5, here.nth(4, 2, 2 * HEADS), 2)
                dve.wait_ge(acc_zero, half + 1)
                for i in range(4):
                    split_w(here, U_HEAD + U_WB + i)
                    for d in range(2):
                        if d:
                            dve.wait_ge(unit_done, here.used(U_HEAD + U_WB + i))
                        else:
                            dve.wait_ge(wb_first, here.nth(i + 1, 4, 16))
                        acc = y_acc[:, 2 * i + d, :]
                        nc.vector.tensor_tensor(acc, acc, proj[d][:], ALU.add).then_inc(proj_free[d], 1)

            for s, n in ((proj_free[0], 1), (proj_free[1], 1), (turn_free[0], 1), (turn_free[1], 1),
                         *((f, 1) for f in wide_free), (rope_done, 1), (pooled, 1)):
                dve.sem_inc(s, n)
            nc.vector.memset(state_all[:], 0.0).then_inc(zeroed, 1)
            nc.vector.memset(history[:], 0.0).then_inc(zeroed, 1)
            for u in range(RING - 1):
                dve.wait_ge(w_hi_s, u + 1)
                rest(w_lo[:, u, :], w_raw[:, u, :], w_hi[:, u, :]).then_inc(w_lo_s, 1)
            dve.wait_ge(zeroed, 2)
            dve.wait_ge(consts_in, 16 * CONSTS)
            with dve.Fori(0, HALVES) as half:
                here = Place(half)
                order = half * ORDER_HALF
                for t in range(TILES):
                    for r in range(2):
                        dve.wait_ge(turn_full, here.turned(2 * t + r))
                        if t:
                            dve.wait_ge(h_lo_s, here.nth(2 * t + r - 1, 0, 2 * TILES))
                        nc.vector.tensor_tensor(
                            h_f[:, r, :].rearrange("p (k s) -> p k s", k=4),
                            turn[r][:].rearrange("p (k s) -> p k s", k=4),
                            gain_in[:, 4 * r:4 * r + 4].rearrange("p (k a) -> p k a", a=1).to_broadcast([P, 4, P]),
                            ALU.mult).then_inc(turn_free[r], 1)
                    for r in range(2):
                        dve.wait_ge(h_hi_s, here.nth(2 * t + r + 1, 0, 2 * TILES))
                        rest(hT_lo[:, 4 * r:4 * r + 4, t * P:(t + 1) * P],
                             h_f[:, r, :].rearrange("p (k s) -> p k s", k=4),
                             hT_hi[:, 4 * r:4 * r + 4, t * P:(t + 1) * P]).then_inc(h_lo_s, 1)
                dve.wait_ge(trig_in, half * 16 + 16)
                for i in range(4):
                    split_w(here, U_KQ + i)
                    if i % 2:
                        rotate(here, J_KQ + i, order + i // 2 * 5, here.nth(1 + i // 2, 0, 2 * HEADS), i - 1)
                with dve.Fori(0, HEADS - 1) as h:
                    head(half, h, False)
                head(half, HEADS - 1, True)
                here = Place(half)
                for i in range(2):
                    dve.wait_ge(proj_free[i], here.proj_read(J_GB - 2 + i))
                nc.vector.tensor_tensor(y_acc[:, 0:4, :], y_acc[:, 0:4, :], kq[:], ALU.mult).then_inc(dve_order, 1)
                for i in range(4):
                    split_w(here, U_GB + i)
                    dve.wait_ge(proj_free[i % 2], here.proj_read(J_GB + i))
                    nc.vector.tensor_tensor(y_acc[:, 4 + i, :], y_acc[:, 4 + i, :], sig[:], ALU.mult)\
                        .then_inc(sig_used, 1)
                with dve.Fori(0, GROUPS) as g:
                    here = at_group(half, g)
                    consts = half * GROUPS + g
                    order = half * ORDER_HALF + g * 8 + (ORDER_POOL + 1)
                    split_w(here, U_POOL)
                    split_w(here, U_POOL + 1)
                    for i in range(2):
                        dve.wait_ge(proj_free[i], here.proj_read(J_POOL + i))
                    past = history[:, g, :].rearrange("p (j s) -> p j s", j=2)
                    nc.vector.tensor_copy(a_in[:, :, 0:HIST], past).then_inc(dve_order, 1)
                    src = a_in
                    for k in range(4):
                        dst = (pa, pb)[k % 2]
                        lo = 2 ** (k + 1) - 1
                        dve.wait_ge(dve_order, order + (k + 1))
                        nc.vector.scalar_tensor_tensor(
                            out=dst[:, :, lo:], in0=src[:, :, lo - 2 ** k:row - 2 ** k],
                            scalar=pool_k[:, consts, k:k + 1], in1=src[:, :, lo:], op0=ALU.mult, op1=ALU.add)\
                            .then_inc(dve_order, 1)
                        src = dst
                    dve.wait_ge(dve_order, order + 5)
                    split_w(here, U_POOL + 2)
                    nc.vector.tensor_tensor(
                        tab_tmp[:].rearrange("p (j s) -> p j s", j=2), src[:, :, HIST:2 * HIST],
                        pool_k[:, consts, 5:5 + 2 * HIST].rearrange("p (j s) -> p j s", j=2), ALU.mult)\
                        .then_inc(dve_order, 1)
                    nc.vector.scalar_tensor_tensor(
                        out=po_f[:, :, HIST:], in0=src[:, :, 2 * HIST:], scalar=pool_k[:, consts, 4:5],
                        in1=a_in[:, :, 2 * HIST:], op0=ALU.mult, op1=ALU.subtract).then_inc(dve_order, 1)
                    nc.vector.tensor_copy(past, a_in[:, :, TOK:]).then_inc(dve_order, 1)
                    dve.wait_ge(dve_order, order + 8)
                    nc.vector.tensor_tensor(po_f[:, :, 0:HIST], tab_tmp[:].rearrange("p (j s) -> p j s", j=2),
                                            a_in[:, :, HIST:2 * HIST], ALU.subtract).then_inc(pooled, 1)
                    dve.wait_ge(wp_hi_s, here.nth(1, 1, GROUPS))
                    rest(wp_lo[:], wp_raw[:, g, :], wp_hi[:]).then_inc(wp_lo_s, 1)
                    for i in range(2):
                        dve.wait_ge(a_sig_s, here.nth(i + 1, 2, 2 * GROUPS))
                        nc.vector.tensor_tensor(a_gate[:, i, :], proj[i][:], a_sig[:, i, :], ALU.mult)\
                            .then_inc(proj_free[i], 1)
                        if i == 0:
                            dve.wait_ge(po_hi_s, here.nth(1, 1, GROUPS))
                            rest(po_lo[:], po_f[:], po_hi[:]).then_inc(po_lo_s, 1)
                            split_w(here, U_POOL + 3)
                    for j in range(2):
                        dve.wait_ge(mix_done, here.nth(j + 1, 2, 2 * GROUPS))
                        nc.vector.scalar_tensor_tensor(
                            out=ya_f[:, j, :], in0=proj[j][:], scalar=scale_k[:, bass.ds(g * 2 + j, 1)],
                            in1=a_gate[:, j, :], op0=ALU.mult, op1=ALU.mult).then_inc(proj_free[j], 1)
                    for j in range(2):
                        dve.wait_ge(ya_hi_s, here.nth(j + 1, 2, 2 * GROUPS))
                        rest(ya_lo[:, g * 2 + j, :], ya_f[:, j, :], ya_hi[:, g * 2 + j, :]).then_inc(ya_lo_s, 1)
                    dve.wait_ge(ya_lo_s, here.nth(2, 2, KT))
                with dve.Fori(0, KT // 2) as i:
                    here = at_merge(half, i)
                    for d in range(2):
                        for n in range(2):
                            split_w(here, U_MERGE + 2 * d + n)
                        if d == 0:
                            dve.wait_ge(sig_used, half * 4 + 4)
                            dve.wait_ge(dve_order, half * ORDER_HALF + ORDER_HALF)
                        dve.wait_ge(proj_free[1], here.proj_read(J_MERGE + 2 * d + 1))
                        nc.vector.tensor_tensor(m_a, proj[0][:], m_sig[:], ALU.mult).then_inc(proj_free[0], 1)
                        dve.wait_ge(proj_free[0], here.proj_read(J_MERGE + 2 * d))
                        nc.vector.tensor_tensor(m_f, m_a, y_acc[:, i * 2 + d, :], ALU.add).then_inc(m_sum, 1)
                        dve.wait_ge(m_hi_s, here.nth(d + 1, 2, KT))
                        rest(m_lo[:, i * 2 + d, :], m_f, m_hi[:, i * 2 + d, :]).then_inc(m_lo_s, 1)
                        dve.wait_ge(m_lo_s, here.nth(d + 1, 2, KT))
                with dve.Fori(0, 2) as e:
                    here = at_out(half, e)
                    for u in range(4):
                        split_w(here, U_OUT + u)
                    dve.wait_ge(unit_done, here.used(U_OUT + 3))
                    for t in range(TILES):
                        dve.wait_ge(x_in[t], half * 32 + 32)
                    for t in range(TILES):
                        xs = x_sb[:, t, bass.ds(e * 512, 512)]
                        nc.vector.tensor_tensor(xs, xs, wide[t][:], ALU.add).then_inc(wide_free[t], 1)
                here = Place(half)
                dve.wait_ge(gain_out_in, half * 16 + 16)
                for t in range(TILES):
                    dve.wait_ge(y_rstd, here.nth(t + 1, 0, TILES))
                    nc.vector.scalar_tensor_tensor(out=x_sb[:, t, :], in0=x_sb[:, t, :], scalar=rstd[:],
                                                   in1=gain_out[:], op0=ALU.mult, op1=ALU.mult).then_inc(y_ready, 1)


def weight_units(w_in, w_a, w_b, w_o):
    offs = np.cumsum((0, 1024, 1024, 1024, 1024, 2048, 2048, 1024, 1024))
    a_in, a_gate, q, k, v, r_gate, g_a, g_b = (w_in[:, offs[i]:offs[i + 1]] for i in range(8))

    def tiles(w, k, e, cols=P):
        rows = w[k[0] * P:k[1] * P, e:e + cols]
        return rows.reshape(k[1] - k[0], P, cols).transpose(1, 0, 2).reshape(P, -1)

    def kq_units(h):
        return [tiles(w, (0, KT), h * DK + j * P) for w in (k, q) for j in range(2)]

    units = kq_units(0)
    for h in range(HEADS):
        units += [tiles(v, (2 * u, 2 * u + 2), h * DV, DV) for u in range(4)]
        units += [tiles(r_gate, (0, KT), h * DV + c * P) for c in range(VT)]
        units += kq_units(h + 1) if h < HEADS - 1 else [tiles(g_b, (0, KT), i * P) for i in range(4)]
        units += [tiles(w_b, (h * VT, (h + 1) * VT), i * 2 * P, 2 * P) for i in range(4)]
    units += [tiles(g_b, (0, KT), (4 + i) * P) for i in range(4)]
    for g in range(GROUPS):
        units += [tiles(w, (0, KT), g * GROUP + j * P) for w in (a_in, a_gate) for j in range(2)]
    for d in range(KT):
        units += [tiles(w_a, (0, KT), d * P), tiles(g_a, (0, KT), d * P)]
    for e in range(2):
        units += [tiles(w_o, (2 * u, 2 * u + 2), e * 512, 512) for u in range(4)]
    assert len(units) == UNITS
    return np.ascontiguousarray(np.stack(units))


def shape_constants():
    half = DK // 2
    inv_freq = (1.0 / (np.float32(ROPE_BASE) ** (np.arange(half, dtype=np.float32) / np.float32(half)))).astype(np.float32)
    angle = np.arange(SEQ, dtype=np.float32)[None, :] * inv_freq[:, None]
    trig = np.stack([np.cos(angle.astype(np.float64)), np.sin(angle.astype(np.float64))], 1)
    trig = trig.reshape(P, 2, HALVES, TOK).transpose(2, 0, 1, 3)

    head = np.zeros((P, HEADS, HC))
    i = np.arange(P)
    for h in range(HEADS):
        gamma = 1.0 - 2.0 ** (-5.0 - h)
        seen = (i[:, None] // CHUNK) <= (i[None, :] // CHUNK)
        head[:, h, 0:P] = seen * gamma ** (np.abs(i[:, None] - i[None, :]) - (i[None, :] + 1.0)) * DK ** -0.5
        head[:, h, P] = gamma ** (P - 1.0 - i) * DK ** -0.5
        head[:, h, P + 1] = EPS / gamma ** (2.0 * (i + 1))
        head[:, h, P + 2] = gamma ** P

    pool = np.zeros((HALVES, GROUPS, PCOLS))
    for s in range(HALVES):
        for g, w in enumerate(WINDOWS):
            pool[s, g, 0:4] = [2 ** k < w for k in range(4)]
            pool[s, g, 4] = 1.0 / w
            pool[s, g, 5:] = np.tile(1.0 / np.minimum(s * TOK + np.arange(HIST) + 1, w), 2)
    pool = np.broadcast_to(pool.reshape(1, HALVES * GROUPS, PCOLS), (P, HALVES * GROUPS, PCOLS))
    return [np.ascontiguousarray(a.astype(np.float32)) for a in (np.eye(P), trig, head, pool)]


def kernel(**inputs):
    import concourse.bacc as bacc
    from concourse.bass_utils import run_bass_kernel_spmd

    a = {n: np.asarray(v) for n, v in inputs.items()}
    ident, trig, head, pool = shape_constants()
    arrays = {
        "wstream": weight_units(a["w_in"], a["w_a"], a["w_b"], a["w_o"]),
        "x": a["x"],
        "norm_in": np.ascontiguousarray(a["norm_in"].reshape(KT, P).T),
        "w_pool": np.ascontiguousarray(a["w_pool"].reshape(GROUPS, 2, P, GROUP).transpose(2, 0, 1, 3)
                                       .reshape(P, GROUPS, 2 * GROUP)),
        "pool_scale": np.ascontiguousarray(a["pool_scale"].reshape(KT, P).T),
        "norm_out": np.ascontiguousarray(np.broadcast_to(a["norm_out"], (P, D_MODEL))),
        "ident": ident, "trig": trig, "head": head, "pool": pool,
    }
    nc = bacc.Bacc("TRN2", target_bir_lowering=False, num_devices=1)
    args = [nc.dram_tensor(f"in_{n}", v.shape, F32, kind="ExternalInput").ap() for n, v in arrays.items()]
    out = nc.dram_tensor("out", (1, SEQ, D_MODEL), F32, kind="ExternalOutput").ap()
    build(nc, *args, out)
    r = run_bass_kernel_spmd(nc, [{f"in_{n}": v for n, v in arrays.items()}], core_ids=[0])
    return r.results[0]["out"]
```

```python
from contextlib import ExitStack

import numpy as np
import concourse.bass as bass
from concourse import mybir

F32 = mybir.dt.float32
F32R = mybir.dt.float32r
ACT = mybir.ActivationFunctionType
ALU = mybir.AluOpType

P = 128
D_MODEL, SEQ = 1024, 1024
HALVES = 2
TOK = SEQ // HALVES
TILES = TOK // P
KT = D_MODEL // P
HEADS, DK, DV = 4, 256, 512
VT = DV // P
CHUNK = 64
WINDOWS = (2, 4, 8, 16)
GROUPS, GROUP = 4, 256
HIST = 16
EPS = 1e-6
ROPE_BASE = 10000.0
RING = 4

U_KQ = 0
U_HEAD = 4
U_V, U_G, U_F, U_WB = 0, 4, 8, 12
U_GB = U_HEAD + 16 * HEADS
U_POOL = U_GB + 4
U_MERGE = U_POOL + 4 * GROUPS
U_OUT = U_MERGE + 2 * KT
UNITS = U_OUT + 8

J_KQ = 0
J_HEAD = 4
J_G, J_F, J_WB = 0, 4, 8
J_GB = J_HEAD + 16 * HEADS
J_POOL = J_GB + 4
J_MERGE = J_POOL + 6 * GROUPS
PROJ_JOBS = J_MERGE + 2 * KT

T_HEAD = 2 * TILES
T_OT = 2 * TILES
TURN_HEAD = T_OT + VT
TURN_JOBS = T_HEAD + TURN_HEAD * HEADS

WIDE_HEAD = (3, 3, 5, 5)
WIDE_HALF = tuple(HEADS * n + 2 for n in WIDE_HEAD)

ORDER_POOL = 10 * HEADS
ORDER_HALF = ORDER_POOL + 1 + 16 * GROUPS
FIRST_CONSTS, CONSTS = 2, 3

TURN_X_AFTER = ((0, 1), (0, 2), (1, 1), (1, 2))

HC = P + 3
PCOLS = 5 + HIST


def build(nc, wstream, x, norm_in, w_pool, pool_scale, norm_out, ident_c, trig_c, head_c, pool_c, out):
    with ExitStack() as ctx:
        def sem(name):
            return ctx.enter_context(nc.semaphore(name))

        top = [(nc.sbuf_base + 31) // 32 * 32]

        def at(name, shape, dt, offset):
            return nc.alloc_sbuf_tensor_at(name, [P, *shape], dt, offset=offset)

        def keep(name, shape, dt=F32):
            t = at(name, shape, dt, top[0])
            top[0] += (4 * int(np.prod(shape)) + 31) // 32 * 32
            return t

        hT_hi, hT_lo = keep("hT_hi", [KT, TOK], F32R), keep("hT_lo", [KT, TOK], F32R)
        w_hi, w_lo = keep("w_hi", [RING, 1024], F32R), keep("w_lo", [RING, 1024], F32R)
        w_raw = keep("w_raw", [RING, 1024])
        state_all = keep("state_all", [HEADS, 2 * DV])
        y_acc = keep("y_acc", [KT, TOK])
        ident = keep("ident", [P])
        trig = keep("trig", [2, TOK])
        head_k = keep("head_k", [HEADS, HC])
        pool_k = keep("pool_k", [HALVES * GROUPS, PCOLS])
        history = keep("history", [GROUPS, 2 * HIST])
        gain_in = keep("gain_in", [KT])
        scale_k = keep("scale_k", [KT])
        ssq, ms, rstd, minus_half, eps_k, eps_head, zeta, inv_dv, inv_dm = (keep(n, [1]) for n in (
            "ssq", "ms", "rstd", "minus_half", "eps_k", "eps_head", "zeta", "inv_dv", "inv_dm"))
        x_ssq, x_rs, y_ssq, y_rs = (keep(n, [TILES]) for n in ("x_ssq", "x_rs", "y_ssq", "y_rs"))
        tab_tmp = keep("tab_tmp", [HIST])

        R, K = top[0], 1024
        v_hi, v_lo = at("v_hi", [TILES, DV], F32R, R), at("v_lo", [TILES, DV], F32R, R + 8 * K)
        yb_hi, yb_lo = at("yb_hi", [VT, TOK], F32R, R + 16 * K), at("yb_lo", [VT, TOK], F32R, R + 24 * K)
        kq = at("kq", [4, TOK], F32, R + 32 * K)
        gate = at("gate", [VT, TOK], F32, R + 40 * K)
        o_n = at("o_n", [TILES, DV], F32, R + 48 * K)
        st_hi, st_lo = at("st_hi", [2, DV], F32R, R + 56 * K), at("st_lo", [2, DV], F32R, R + 60 * K)
        state = at("state", [2, DV], F32, R + 64 * K)
        rope_in = at("rope_in", [2, TOK], F32, R + 68 * K)
        pair = at("pair", [2, TOK], F32, R + 72 * K)
        sig = at("sig", [TOK], F32, R + 76 * K)
        junk = at("junk", [DV], F32, R + 78 * K)
        sc_f, sc_hi, sc_lo = (at(n, [P], d, R + 80 * K + i * 512) for i, (n, d) in enumerate(
            (("sc_f", F32), ("sc_hi", F32R), ("sc_lo", F32R))))
        kn_f, kn_hi, kn_lo, q_hi, q_lo = (at(n, [DK], d, R + 81 * K + 512 + i * K) for i, (n, d) in enumerate(
            (("kn_f", F32), ("kn_hi", F32R), ("kn_lo", F32R), ("q_hi", F32R), ("q_lo", F32R))))
        h_f = at("h_f", [2, TOK], F32, R)
        h_junk = at("h_junk", [D_MODEL], F32, R + 4 * K)
        x_sb = at("x_sb", [TILES, D_MODEL], F32, R + 64 * K)
        ya_hi, ya_lo = at("ya_hi", [KT, TOK], F32R, R), at("ya_lo", [KT, TOK], F32R, R + 16 * K)
        row = HIST + TOK
        a_in, pa, pb = (at(n, [2, row], F32, R + 32 * K + i * 8 * row) for i, n in enumerate(("a_in", "pa", "pb")))
        po_f, po_hi, po_lo = (at(n, [2, TOK], d, R + 45 * K + 4 * K * i) for i, (n, d) in enumerate(
            (("po_f", F32), ("po_hi", F32R), ("po_lo", F32R))))
        wp_hi, wp_lo = at("wp_hi", [2 * GROUP], F32R, R + 57 * K), at("wp_lo", [2 * GROUP], F32R, R + 59 * K)
        wp_raw = at("wp_raw", [GROUPS, 2 * GROUP], F32, R + 64 * K)
        a_sig, a_gate, ya_f = (at(n, [2, TOK], F32, R + (72 + 4 * i) * K) for i, n in enumerate(
            ("a_sig", "a_gate", "ya_f")))
        m_hi, m_lo = at("m_hi", [KT, TOK], F32R, R + 32 * K), at("m_lo", [KT, TOK], F32R, R + 48 * K)
        y = at("y", [TILES, D_MODEL], F32, R + 16 * K)
        gain_out = at("gain_out", [D_MODEL], F32, R + 80 * K)
        m_sig = at("m_sig", [TOK], F32, R + 84 * K)
        m_f, m_a = trig[:, 0, :], trig[:, 1, :]
        out_junk = at("out_junk", [D_MODEL], F32, R + 8 * K)
        assert R + 86 * K + 512 <= nc.sbuf_usable_end, R

        proj = [ctx.enter_context(nc.psum_tensor(f"proj{i}", [P, 512], F32)) for i in range(2)]
        wide = [ctx.enter_context(nc.psum_tensor(f"wide{i}", [P, 512], F32)) for i in range(4)]
        turn = [ctx.enter_context(nc.psum_tensor(f"turn{i}", [P, 512], F32)) for i in range(2)]

        first_consts_in, consts_in = sem("first_consts_in"), sem("consts_in")
        raw_in = [sem(f"raw_in{i}") for i in range(RING)]
        x_in = [sem(f"x_in{i}") for i in range(TILES)]
        trig_in, wp_in, y_in = sem("trig_in"), sem("wp_in"), sem("y_in")
        stored = sem("stored")
        unit_done = sem("unit_done")
        wb_first = sem("wb_first")
        mix_done = sem("mix_done")
        turn_full = sem("turn_full")
        o_full, upd_full = sem("o_full"), sem("upd_full")
        out_full = sem("out_full")
        proj_free = [sem(f"proj_free{i}") for i in range(2)]
        turn_free = [sem(f"turn_free{i}") for i in range(2)]
        wide_free = [sem(f"wide_free{i}") for i in range(4)]
        w_hi_s, w_lo_s = sem("w_hi_ready"), sem("w_lo_ready")
        h_hi_s, h_lo_s = sem("h_hi_ready"), sem("h_lo_ready")
        v_hi_s, q_hi_s, q_lo_s = sem("v_hi_ready"), sem("q_hi_ready"), sem("q_lo_ready")
        sc_hi_s, sc_lo_s = sem("sc_hi_ready"), sem("sc_lo_ready")
        kn_hi_s, kn_lo_s = sem("kn_hi_ready"), sem("kn_lo_ready")
        st_hi_s, st_lo_s = sem("st_hi_ready"), sem("st_lo_ready")
        yb_hi_s, yb_lo_s = sem("yb_hi_ready"), sem("yb_lo_ready")
        po_hi_s, po_lo_s = sem("po_hi_ready"), sem("po_lo_ready")
        wp_hi_s, wp_lo_s = sem("wp_hi_ready"), sem("wp_lo_ready")
        ya_hi_s, ya_lo_s = sem("ya_hi_ready"), sem("ya_lo_ready")
        m_hi_s, m_lo_s = sem("m_hi_ready"), sem("m_lo_ready")
        x_sq, x_rstd, x_scaled = sem("x_sq"), sem("x_rstd"), sem("x_scaled")
        o_sq, o_rstd = sem("o_sq"), sem("o_rstd")
        y_sq, y_rstd, y_ready = sem("y_sq"), sem("y_rstd"), sem("y_ready")
        rope_done = sem("rope_done")
        gate_sig, sig_used, a_sig_s = sem("gate_sig"), sem("sig_used"), sem("a_sig_ready")
        pooled = sem("pooled")
        m_sum = sem("m_sum")
        acc_zero = sem("acc_zero")
        dve_order, pool_order = sem("dve_order"), sem("pool_order")
        zeroed = sem("zeroed")
        zeta_ready = sem("zeta_ready")
        merged = sem("merged")

        x_t = x.rearrange("b (h t p) d -> (b h) t p d", h=HALVES, t=TILES)
        out_t = out.rearrange("b (h t p) d -> (b h) t p d", h=HALVES, t=TILES)

        block = ctx.enter_context(nc.Block())

        class Place:

            def __init__(self, half, s=0, units=0, projs=0):
                self.half, self.s, self.units, self.projs = half, s, units, projs

            def split(self, u):
                return self.half * UNITS + self.s * self.units + (u + 1)

            def used(self, u):
                return self.half * UNITS + self.s * self.units + (u + 2)

            def loaded(self, u):
                return self.half * (16 * UNITS // RING) + self.s * (16 * self.units // RING) + 16 * (u // RING + 1)

            def proj_open(self, j):
                return self.half * (PROJ_JOBS // 2) + self.s * (self.projs // 2) + (j // 2 + 1)

            def proj_read(self, j):
                return self.proj_open(j) + 1

            def turn_open(self, j):
                return self.half * (TURN_JOBS // 2) + self.s * (TURN_HEAD // 2) + (j // 2 + 1)

            def turn_read(self, j):
                return self.turn_open(j) + 1

            def turned(self, j):
                return self.half * TURN_JOBS + self.s * TURN_HEAD + (j + 1)

            def wide_open(self, b, n):
                return self.half * WIDE_HALF[b] + self.s * WIDE_HEAD[b] + (n + 1)

            def nth(self, n, per_step, per_half):
                return self.half * per_half + self.s * per_step + n

        def at_head(half, h):
            return Place(half, h, 16, 16)

        def at_group(half, g):
            return Place(half, g, 4, 6)

        def at_merge(half, i):
            return Place(half, i, 4, 4)

        @block.sync
        def _(sp):
            sp.dma_start(x_sb[:, 0, :], x_t[0, 0]).then_inc(x_in[0], 16)
            sp.dma_start(ident[:], ident_c).then_inc(first_consts_in, 16)
            sp.dma_start(gain_in[:], norm_in).then_inc(first_consts_in, 16)
            for t in range(1, TILES):
                sp.dma_start(x_sb[:, t, :], x_t[0, t]).then_inc(x_in[t], 16)
            for r in range(RING):
                sp.dma_start(w_raw[:, r, :], wstream[r]).then_inc(raw_in[r], 16)
            sp.dma_start(trig[:], trig_c[0]).then_inc(trig_in, 16)
            sp.dma_start(head_k[:], head_c).then_inc(consts_in, 16)
            sp.dma_start(pool_k[:], pool_c).then_inc(consts_in, 16)
            sp.dma_start(scale_k[:], pool_scale).then_inc(consts_in, 16)

            def load_units(half, first, last):
                with sp.Fori(first // RING, last // RING) as q:
                    for r in range(RING):
                        sp.wait_ge(w_lo_s, half * UNITS + q * RING + (r + 1))
                        sp.dma_start(w_raw[:, r, :], wstream[q * RING + (RING + r)]).then_inc(raw_in[r], 16)

            with sp.Fori(0, HALVES) as half:
                here = Place(half)
                load_units(half, 0, U_POOL)
                sp.wait_ge(sig_used, here.nth(4, 0, 4))
                sp.dma_start(wp_raw[:], w_pool).then_inc(wp_in, 16)
                load_units(half, U_POOL, U_MERGE)
                sp.wait_ge(ya_lo_s, here.nth(KT, 0, KT))
                for t in range(TILES):
                    sp.dma_start(x_sb[:, t, :], x_t[HALVES - 1, t]).then_inc(x_in[t], 16)
                load_units(half, U_MERGE, U_OUT)
                sp.wait_ge(unit_done, here.used(U_OUT - 1))
                for t in range(TILES):
                    sp.dma_start(y[:, t, :], x_t[half, t]).then_inc(y_in, 16)
                sp.dma_start(gain_out[:], norm_out).then_inc(y_in, 16)
                load_units(half, U_OUT, UNITS - RING)
                for r in range(RING):
                    sp.wait_ge(w_lo_s, here.split(UNITS - RING + r))
                    sp.dma_start(w_raw[:, r, :], wstream[r]).then_inc(raw_in[r], 16)
                sp.wait_ge(m_lo_s, here.nth(KT, 0, KT))
                sp.dma_start(trig[:], trig_c[HALVES - 1]).then_inc(trig_in, 16)
                for t in range(TILES):
                    sp.wait_ge(y_ready, here.nth(t + 1, 0, TILES))
                    sp.dma_start(out_t[half, t], y[:, t, :]).then_inc(stored, 16)
            sp.wait_ge(stored, 16 * TILES * HALVES)
            for t in range(TILES):
                sp.wait_ge(x_in[t], 16 * (HALVES + 1))
            sp.wait_ge(trig_in, 16 * (HALVES + 1))
            for r in range(RING):
                sp.wait_ge(raw_in[r], 16 * (HALVES * UNITS // RING + 1))

        @block.tensor
        def _(pe):
            def mm3(dst, a_hi, a_lo, b_hi, b_lo, first, last):
                nc.tensor.matmul(dst, a_hi, b_hi, start=first, stop=False)
                nc.tensor.matmul(dst, a_hi, b_lo, start=False, stop=False)
                return nc.tensor.matmul(dst, a_lo, b_hi, start=False, stop=last)

            def slot(u, k):
                s = u % RING
                return (w_hi[:, s, :].rearrange("p (k e) -> p k e", k=k),
                        w_lo[:, s, :].rearrange("p (k e) -> p k e", k=k))

            def project(here, u, j, b_hi, b_lo):
                pe.wait_ge(w_lo_s, here.split(u))
                pe.wait_ge(proj_free[j % 2], here.proj_open(j))
                wh, wl = slot(u, KT)
                for k in range(KT):
                    mm = mm3(proj[j % 2][:], wh[:, k, :], wl[:, k, :], b_hi[:, k, :], b_lo[:, k, :],
                             k == 0, k == KT - 1)
                mm.then_inc(unit_done, 1)

            def natural(here, u, n, a_hi, a_lo):
                pe.wait_ge(w_lo_s, here.split(u))
                wh, wl = slot(u, 2)
                for t in range(TILES):
                    cols = slice(t * P, (t + 1) * P)
                    for k in range(2):
                        mm = mm3(wide[t][:], a_hi[:, 2 * n + k, cols], a_lo[:, 2 * n + k, cols],
                                 wh[:, k, :], wl[:, k, :], n == 0 and k == 0, n == 3 and k == 1)
                mm.then_inc(unit_done, 1)

            def head(half, h):
                here = at_head(half, h)
                for b in range(4):
                    pe.wait_ge(wide_free[b], here.wide_open(b, 0))
                for u in range(4):
                    natural(here, U_HEAD + U_V + u, u, hT_hi, hT_lo)
                pe.wait_ge(rope_done, here.nth(3, 2, 2 * HEADS))
                for t in range(TILES):
                    cols = slice(t * P, (t + 1) * P)
                    pe.wait_ge(turn_free[0], here.turn_open(T_HEAD + 2 * t))
                    for j in range(2):
                        mm = nc.tensor.matmul(turn[0][:, 0:P], kq[:, j, cols], kq[:, 2 + j, cols],
                                              start=j == 0, stop=j == 1)
                    mm.then_inc(turn_full, 1)
                    pe.wait_ge(turn_free[1], here.turn_open(T_HEAD + 2 * t + 1))
                    for j in range(2):
                        mm = nc.tensor.transpose(turn[1][:, j * P:(j + 1) * P], kq[:, j, cols], ident[:])
                    mm.then_inc(turn_full, 1)
                    project(here, U_HEAD + U_G + t, J_HEAD + J_G + t, hT_hi, hT_lo)
                    o = wide[t % 2]
                    pe.wait_ge(wide_free[t % 2], here.wide_open(t % 2, 1 + t // 2))
                    pe.wait_ge(sc_lo_s, here.nth(t + 1, 4, 16))
                    mm3(o[:], sc_hi[:], sc_lo[:], v_hi[:, t, :], v_lo[:, t, :], True, False)
                    pe.wait_ge(q_lo_s, here.nth(t + 1, 4, 16))
                    pe.wait_ge(st_lo_s, here.nth(t + 1, 4, 16))
                    for j in range(2):
                        mm = mm3(o[:], q_hi[:, j * P:(j + 1) * P], q_lo[:, j * P:(j + 1) * P],
                                 st_hi[:, j, :], st_lo[:, j, :], False, j == 1)
                    mm.then_inc(o_full, 1)
                    pe.wait_ge(kn_lo_s, here.nth(t + 1, 4, 16))
                    for j in range(2):
                        pe.wait_ge(wide_free[2 + j], here.wide_open(2 + j, 1 + t))
                        mm = mm3(wide[2 + j][:], kn_hi[:, j * P:(j + 1) * P], kn_lo[:, j * P:(j + 1) * P],
                                 v_hi[:, t, :], v_lo[:, t, :], True, True)
                    mm.then_inc(upd_full, 1)

                def filler(i):
                    project(here, U_HEAD + U_F + i, J_HEAD + J_F + i, hT_hi, hT_lo)

                def turn_o(c):
                    pe.wait_ge(turn_free[c % 2], here.turn_open(T_HEAD + T_OT + c))
                    for t in range(TILES):
                        mm = nc.tensor.transpose(turn[c % 2][:, t * P:(t + 1) * P],
                                                 o_n[:, t, c * P:(c + 1) * P], ident[:])
                    mm.then_inc(turn_full, 1)

                filler(0)
                for b in range(2):
                    pe.wait_ge(wide_free[b], here.wide_open(b, 3))
                turn_o(0)
                turn_o(1)
                filler(1)
                turn_o(2)
                turn_o(3)
                filler(2)
                filler(3)
                pe.wait_ge(yb_lo_s, here.nth(VT, VT, HEADS * VT))
                for i in range(4):
                    u = U_HEAD + U_WB + i
                    pe.wait_ge(w_lo_s, here.split(u))
                    wh, wl = slot(u, VT)
                    for d in range(2):
                        pe.wait_ge(proj_free[d], here.proj_open(J_HEAD + J_WB + 2 * i + d))
                        for k in range(VT):
                            mm = mm3(proj[d][:], wh[:, k, d * P:(d + 1) * P], wl[:, k, d * P:(d + 1) * P],
                                     yb_hi[:, k, :], yb_lo[:, k, :], k == 0, k == VT - 1)
                        mm.then_inc(unit_done if d else wb_first, 1)

            def turn_x(here, t):
                pe.wait_ge(x_scaled, here.nth(t + 1, 0, TILES))
                for r in range(2):
                    pe.wait_ge(turn_free[r], here.turn_open(2 * t + r))
                    for k in range(4):
                        d = (4 * r + k) * P
                        mm = nc.tensor.transpose(turn[r][:, k * P:(k + 1) * P], x_sb[:, t, d:d + P], ident[:])
                    mm.then_inc(turn_full, 1)

            pe.sem_inc(unit_done, 1)
            pe.wait_ge(first_consts_in, 16 * FIRST_CONSTS)
            for t in range(TILES):
                turn_x(Place(0), t)
            with pe.Fori(0, HALVES) as half:
                here = Place(half)
                pe.wait_ge(h_lo_s, here.nth(2 * TILES, 0, 2 * TILES))
                for i in range(4):
                    project(here, U_KQ + i, J_KQ + i, hT_hi, hT_lo)
                with pe.Fori(0, HEADS - 1) as h:
                    head(half, h)
                head(half, HEADS - 1)
                for i in range(4):
                    project(here, U_GB + i, J_GB + i, hT_hi, hT_lo)
                with pe.Fori(0, GROUPS) as g:
                    here = at_group(half, g)
                    for i in range(4):
                        project(here, U_POOL + i, J_POOL + i, hT_hi, hT_lo)
                    pe.wait_ge(wp_lo_s, here.nth(1, 1, GROUPS))
                    pe.wait_ge(po_lo_s, here.nth(2, 2, 2 * GROUPS))
                    for j in range(2):
                        pe.wait_ge(proj_free[j], here.proj_open(J_POOL + 4 + j))
                        for k in range(2):
                            e = k * GROUP + j * P
                            mm = mm3(proj[j][:], wp_hi[:, e:e + P], wp_lo[:, e:e + P],
                                     po_hi[:, k, :], po_lo[:, k, :], k == 0, k == 1)
                        mm.then_inc(mix_done, 1)
                with pe.Fori(0, KT // 2) as i:
                    here = at_merge(half, i)
                    for d in range(2):
                        project(here, U_MERGE + 2 * d, J_MERGE + 2 * d, hT_hi, hT_lo)
                        pe.wait_ge(ya_lo_s, Place(half).nth(KT, 0, KT))
                        project(here, U_MERGE + 2 * d + 1, J_MERGE + 2 * d + 1, ya_hi, ya_lo)
                here = Place(half)
                for e in range(2):
                    for t in range(TILES):
                        cols = slice(t * P, (t + 1) * P)
                        pe.wait_ge(wide_free[t], half * WIDE_HALF[t] + (WIDE_HALF[t] - 1 + e))
                        for n in range(4):
                            u = U_OUT + 4 * e + n
                            if t == 0:
                                pe.wait_ge(w_lo_s, here.split(u))
                                if e == 0:
                                    pe.wait_ge(m_lo_s, here.nth(2 * n + 2, 0, KT))
                            wh, wl = slot(u, 2)
                            for k in range(2):
                                mm = mm3(wide[t][:], m_hi[:, 2 * n + k, cols], m_lo[:, 2 * n + k, cols],
                                         wh[:, k, :], wl[:, k, :], n == 0 and k == 0, n == 3 and k == 1)
                            if t == TILES - 1:
                                mm.then_inc(unit_done, 1)
                        if t < TILES - 1:
                            mm.then_inc(out_full, 1)
                        if (e, t) in TURN_X_AFTER:
                            turn_x(Place(half + 1), TURN_X_AFTER.index((e, t)))

        @block.scalar
        def _(act):
            def copy(dst, src):
                return nc.scalar.activation(dst, src, ACT.Copy)

            def split_w(here, u):
                s = (u + 3) % RING
                act.wait_ge(raw_in[s], here.loaded(u + 3))
                act.wait_ge(unit_done, here.used(u - 1))
                copy(w_hi[:, s, :], w_raw[:, s, :]).then_inc(w_hi_s, 1)

            def rope_copy(here, u, j, rope):
                act.wait_ge(unit_done, here.used(u))
                if j % 2 == 0:
                    act.wait_ge(rope_done, rope)
                copy(rope_in[:, j % 2, :], proj[j % 2][:]).then_inc(proj_free[j % 2], 1)

            def head(half, h, closing):
                here = at_head(half, h)
                copy(zeta[:], head_k[:, h, P:P + 1]).then_inc(zeta_ready, 1)
                for u in range(4):
                    split_w(here, U_HEAD + U_V + u)
                act.wait_ge(unit_done, here.used(U_HEAD + U_V + 3))
                copy(st_hi[:].rearrange("p j e -> p (j e)"), state_all[:, h, :]).then_inc(st_hi_s, 1)
                for t in range(TILES):
                    copy(v_hi[:, t, :], wide[t][:]).then_inc(v_hi_s, 1)
                act.wait_ge(zeta_ready, here.nth(1, 1, HEADS))
                act.wait_ge(rope_done, here.nth(3, 2, 2 * HEADS))
                for t in range(TILES):
                    cols = slice(t * P, (t + 1) * P)
                    if t:
                        act.wait_ge(o_full, here.nth(t, 4, 16))
                        act.wait_ge(q_lo_s, here.nth(t, 4, 16))
                    copy(q_hi[:].rearrange("p (j s) -> p j s", j=2), kq[:, 2:4, cols]).then_inc(q_hi_s, 1)
                    act.wait_ge(turn_free[0], here.turn_read(T_HEAD + 2 * t))
                    copy(sc_hi[:], sc_f[:]).then_inc(sc_hi_s, 1)
                    act.wait_ge(turn_full, here.turned(T_HEAD + 2 * t + 1))
                    if t:
                        act.wait_ge(upd_full, here.nth(t, 4, 16))
                        act.wait_ge(kn_lo_s, here.nth(t, 4, 16))
                    nc.scalar.activation(kn_f[:], turn[1][:, 0:DK], ACT.Copy,
                                         scale=zeta[:]).then_inc(turn_free[1], 1)
                    act.wait_ge(turn_free[1], here.turn_read(T_HEAD + 2 * t + 1))
                    copy(kn_hi[:], kn_f[:]).then_inc(kn_hi_s, 1)
                    split_w(here, U_HEAD + U_G + t)
                    act.wait_ge(unit_done, here.used(U_HEAD + U_G + t))
                    if t:
                        act.wait_ge(proj_free[(t - 1) % 2], here.proj_read(J_HEAD + J_G + t - 1))
                    nc.scalar.activation(sig[:], proj[t % 2][:], ACT.Sigmoid).then_inc(gate_sig, 1)
                    act.wait_ge(o_full, here.nth(t + 1, 4, 16))
                    nc.scalar.activation(junk[:], wide[t % 2][:], ACT.Square, accum_out=ssq[:]).then_inc(o_sq, 1)
                    if t < TILES - 1:
                        for j in range(2):
                            act.wait_ge(wide_free[2 + j], here.wide_open(2 + j, 2 + t))
                        copy(st_hi[:], state[:]).then_inc(st_hi_s, 1)
                    act.wait_ge(o_rstd, here.nth(t + 1, 4, 16))
                    nc.scalar.activation(o_n[:, t, :], wide[t % 2][:], ACT.Copy,
                                         scale=rstd[:]).then_inc(wide_free[t % 2], 1)

                def filled(i):
                    u, j = U_HEAD + U_F + i, J_HEAD + J_F + i
                    if closing:
                        act.wait_ge(unit_done, here.used(u))
                        nc.scalar.activation(kq[:, i, :], proj[i % 2][:], ACT.Sigmoid).then_inc(proj_free[i % 2], 1)
                    else:
                        rope_copy(here, u, j, here.nth(3 + i // 2, 2, 2 * HEADS))

                def split_yb(c):
                    act.wait_ge(turn_free[c % 2], here.turn_read(T_HEAD + T_OT + c))
                    copy(yb_hi[:, c, :], pair[:, c % 2, :]).then_inc(yb_hi_s, 1)

                split_w(here, U_HEAD + U_F)
                filled(0)
                split_yb(0)
                split_yb(1)
                split_w(here, U_HEAD + U_F + 1)
                filled(1)
                split_yb(2)
                split_yb(3)
                for i in (2, 3):
                    split_w(here, U_HEAD + U_F + i)
                    filled(i)
                for i in range(4):
                    split_w(here, U_HEAD + U_WB + i)

            def x_square(here, t):
                act.wait_ge(x_in[t], here.half * 16 + 16)
                nc.scalar.activation(h_junk[:], x_sb[:, t, :], ACT.Square, accum_out=x_ssq[:, t:t + 1])\
                    .then_inc(x_sq, 1)

            def x_scale(here, t):
                act.wait_ge(x_rstd, here.nth(t + 1, 0, TILES))
                nc.scalar.activation(x_sb[:, t, :], x_sb[:, t, :], ACT.Copy, scale=x_rs[:, t:t + 1])\
                    .then_inc(x_scaled, 1)

            def split_h(here, t):
                for r in range(2):
                    act.wait_ge(turn_free[r], here.turn_read(2 * t + r))
                    copy(hT_hi[:, 4 * r:4 * r + 4, t * P:(t + 1) * P],
                         h_f[:, r, :].rearrange("p (k s) -> p k s", k=4)).then_inc(h_hi_s, 1)

            def first_split(u):
                act.wait_ge(raw_in[u], 16)
                copy(w_hi[:, u, :], w_raw[:, u, :]).then_inc(w_hi_s, 1)

            def y_square(here, t):
                act.wait_ge(wide_free[t], here.wide_open(t, WIDE_HALF[t]))
                act.wait_ge(y_sq, here.nth(t + 1, 0, TILES))
                nc.scalar.activation(out_junk[:], y[:, t, :], ACT.Square, accum_out=y_ssq[:, t:t + 1])\
                    .then_inc(y_sq, 1)

            first = Place(0)
            act.sem_inc(x_sq, 1)
            act.sem_inc(y_sq, 1)
            x_square(first, 0)
            for t in range(1, TILES):
                act.wait_ge(x_sq, t + 1)
                x_square(first, t)
                x_scale(first, t - 1)
                if t > 1:
                    split_h(first, t - 2)
            x_scale(first, TILES - 1)
            first_split(0)
            split_h(first, TILES - 2)
            first_split(1)
            split_h(first, TILES - 1)
            first_split(2)
            act.wait_ge(consts_in, 16 * CONSTS)
            with act.Fori(0, HALVES) as half:
                here = Place(half)
                for i in range(4):
                    split_w(here, U_KQ + i)
                    rope_copy(here, U_KQ + i, J_KQ + i, here.nth(1 + i // 2, 2, 2 * HEADS))
                with act.Fori(0, HEADS - 1) as h:
                    head(half, h, False)
                head(half, HEADS - 1, True)
                for i in range(4):
                    split_w(here, U_GB + i)
                    act.wait_ge(unit_done, here.used(U_GB + i))
                    if i:
                        act.wait_ge(sig_used, here.nth(i, 0, 4))
                    nc.scalar.activation(sig[:], proj[i % 2][:], ACT.Sigmoid).then_inc(proj_free[i % 2], 1)
                with act.Fori(0, GROUPS) as g:
                    here = at_group(half, g)
                    for i in range(2):
                        split_w(here, U_POOL + i)
                        act.wait_ge(unit_done, here.used(U_POOL + i))
                        act.wait_ge(pooled, here.nth(1 + i, 2, 2 * GROUPS))
                        copy(a_in[:, i, HIST:], proj[i][:]).then_inc(proj_free[i], 1)
                    act.wait_ge(wp_in, half * 16 + 16)
                    copy(wp_hi[:], wp_raw[:, g, :]).then_inc(wp_hi_s, 1)
                    for i in range(2):
                        split_w(here, U_POOL + 2 + i)
                        act.wait_ge(unit_done, here.used(U_POOL + 2 + i))
                        nc.scalar.activation(a_sig[:, i, :], proj[i][:], ACT.Sigmoid).then_inc(a_sig_s, 1)
                        act.wait_ge(pooled, here.nth(2 + i, 2, 2 * GROUPS))
                        copy(po_hi[:, i, :], po_f[:, i, :]).then_inc(po_hi_s, 1)
                    for j in range(2):
                        act.wait_ge(proj_free[j], here.proj_read(J_POOL + 4 + j))
                        copy(ya_hi[:, g * 2 + j, :], ya_f[:, j, :]).then_inc(ya_hi_s, 1)
                with act.Fori(0, KT // 2) as i:
                    here = at_merge(half, i)
                    for d in range(2):
                        split_w(here, U_MERGE + 2 * d)
                        act.wait_ge(unit_done, here.used(U_MERGE + 2 * d))
                        nc.scalar.activation(m_sig[:], proj[0][:], ACT.Sigmoid).then_inc(proj_free[0], 1)
                        split_w(here, U_MERGE + 2 * d + 1)
                        act.wait_ge(m_sum, here.nth(d + 1, 2, KT))
                        copy(m_hi[:, i * 2 + d, :], m_f).then_inc(m_hi_s, 1)
                here, after = Place(half), Place(half + 1)
                split_w(here, U_OUT)
                for t in range(TILES):
                    act.wait_ge(x_sq, after.nth(t + 1, 0, TILES))
                    x_square(after, t)
                    if t:
                        x_scale(after, t - 1)
                x_scale(after, TILES - 1)
                split_h(after, 0)
                split_h(after, 1)
                for u in range(1, 5):
                    split_w(here, U_OUT + u)
                y_square(here, 0)
                split_h(after, 2)
                y_square(here, 1)
                split_h(after, 3)
                y_square(here, 2)
                for u in range(5, 8):
                    split_w(here, U_OUT + u)
                y_square(here, 3)

        @block.gpsimd
        def _(pool):
            count = [0]

            def link(ins, base):
                count[0] += 1
                ins.then_inc(pool_order, 1)
                pool.wait_ge(pool_order, base + count[0])

            def rms(dst, src, base, inv_n, eps):
                count[0] = 0
                link(nc.gpsimd.tensor_tensor(ms[:], src, inv_n[:], ALU.mult), base)
                link(nc.gpsimd.tensor_tensor(ms[:], ms[:], eps[:], ALU.add), base)
                return nc.gpsimd.tensor_tensor(dst, ms[:], minus_half[:], ALU.pow)

            def x_rms(here, base):
                for t in range(TILES):
                    pool.wait_ge(x_sq, here.nth(t + 2, 0, TILES))
                    if t:
                        pool.wait_ge(x_rstd, here.nth(t, 0, TILES))
                    rms(x_rs[:, t:t + 1], x_ssq[:, t:t + 1], base + 2 * t, inv_dm, eps_k).then_inc(x_rstd, 1)

            for t, value in ((minus_half, -0.5), (eps_k, EPS), (inv_dm, 1.0 / D_MODEL), (inv_dv, 1.0 / DV)):
                nc.gpsimd.memset(t[:], value).then_inc(pool_order, 1)
            pool.wait_ge(pool_order, 4)
            x_rms(Place(0), 4)
            nc.gpsimd.memset(y_acc[:], 0.0).then_inc(acc_zero, 1)
            pool.wait_ge(consts_in, 16 * CONSTS)
            pool.sem_inc(merged, 1)
            rows, head_part = 2 * TILES, 2 * TILES + 1
            with pool.Fori(0, HALVES) as half:
                here = Place(half)
                order = half * (2 * rows + HEADS * head_part) + (4 + rows)
                with pool.Fori(0, HEADS) as h:
                    nc.gpsimd.tensor_copy(eps_head[:], head_k[:, h, P + 1:P + 2]).then_inc(pool_order, 1)
                    pool.wait_ge(pool_order, order + h * head_part + 1)
                    for t in range(TILES):
                        pool.wait_ge(o_sq, at_head(half, h).nth(t + 1, 4, 16))
                        rms(rstd[:], ssq[:], order + h * head_part + (1 + 2 * t), inv_dv, eps_head).then_inc(o_rstd, 1)
                order = order + HEADS * head_part
                x_rms(Place(half + 1), order)
                pool.wait_ge(m_sum, here.nth(KT, 0, KT))
                pool.sem_inc(merged, 1)
                nc.gpsimd.memset(y_acc[:], 0.0).then_inc(acc_zero, 1)
                for t in range(TILES):
                    pool.wait_ge(y_sq, here.nth(t + 2, 0, TILES))
                    if t:
                        pool.wait_ge(y_rstd, here.nth(t, 0, TILES))
                    rms(y_rs[:, t:t + 1], y_ssq[:, t:t + 1], order + (rows + 2 * t), inv_dm, eps_k).then_inc(y_rstd, 1)

        @block.vector
        def _(dve):
            def rest(dst, src, hi):
                return nc.vector.tensor_tensor(dst, src, hi.bitcast(F32), ALU.subtract)

            def split_w(here, u):
                s = (u + 3) % RING
                dve.wait_ge(w_hi_s, here.split(u + 3))
                rest(w_lo[:, s, :], w_raw[:, s, :], w_hi[:, s, :]).then_inc(w_lo_s, 1)

            def rotate(here, part, j, order, done, n):
                if part == 0:
                    for i in range(2):
                        dve.wait_ge(proj_free[i], here.proj_read(j - 1 + i))
                    dve.wait_ge(rope_done, done)
                else:
                    dve.wait_ge(dve_order, order + 3)
                cos, sin = trig[:, 0, :], trig[:, 1, :]
                first, second, op = ((cos, sin, ALU.subtract), (sin, cos, ALU.add))[part]
                nc.vector.tensor_tensor(pair[:, 0, :], rope_in[:, 0, :], first, ALU.mult).then_inc(dve_order, 1)
                nc.vector.tensor_tensor(pair[:, 1, :], rope_in[:, 1, :], second, ALU.mult).then_inc(dve_order, 1)
                dve.wait_ge(dve_order, order + 3 * part + 2)
                nc.vector.tensor_tensor(kq[:, n + part, :], pair[:, 0, :], pair[:, 1, :], op)\
                    .then_inc(rope_done if part else dve_order, 1)

            def head(half, h, closing):
                here = at_head(half, h)
                for u in range(4):
                    split_w(here, U_HEAD + U_V + u)
                dve.wait_ge(st_hi_s, here.nth(1, 4, 16))
                rest(st_lo[:].rearrange("p j e -> p (j e)"), state_all[:, h, :],
                     st_hi[:].rearrange("p j e -> p (j e)")).then_inc(st_lo_s, 1)
                for t in range(TILES):
                    dve.wait_ge(v_hi_s, here.nth(t + 1, 4, 16))
                    rest(v_lo[:, t, :], wide[t][:], v_hi[:, t, :]).then_inc(wide_free[t], 1)
                for t in range(TILES):
                    cols = slice(t * P, (t + 1) * P)
                    dve.wait_ge(turn_full, here.turned(T_HEAD + 2 * t))
                    nc.vector.tensor_tensor(sc_f[:], turn[0][:, 0:P], head_k[:, h, 0:P], ALU.mult)\
                        .then_inc(turn_free[0], 1)
                    dve.wait_ge(q_hi_s, here.nth(t + 1, 4, 16))
                    rest(q_lo[:].rearrange("p (j s) -> p j s", j=2), kq[:, 2:4, cols],
                         q_hi[:].rearrange("p (j s) -> p j s", j=2)).then_inc(q_lo_s, 1)
                    dve.wait_ge(sc_hi_s, here.nth(t + 1, 4, 16))
                    rest(sc_lo[:], sc_f[:], sc_hi[:]).then_inc(sc_lo_s, 1)
                    dve.wait_ge(kn_hi_s, here.nth(t + 1, 4, 16))
                    rest(kn_lo[:], kn_f[:], kn_hi[:]).then_inc(kn_lo_s, 1)
                    split_w(here, U_HEAD + U_G + t)
                    dve.wait_ge(gate_sig, here.nth(t + 1, 4, 16))
                    nc.vector.tensor_tensor(gate[:, t, :], proj[t % 2][:], sig[:], ALU.mult)\
                        .then_inc(proj_free[t % 2], 1)
                    dve.wait_ge(upd_full, here.nth(t + 1, 4, 16))
                    for j in range(2):
                        kept = state_all[:, h, j * DV:(j + 1) * DV]
                        nc.vector.scalar_tensor_tensor(
                            out=kept if t == TILES - 1 else state[:, j, :], in0=kept if t == 0 else state[:, j, :],
                            scalar=head_k[:, h, P + 2:P + 3], in1=wide[2 + j][:], op0=ALU.mult, op1=ALU.add)\
                            .then_inc(wide_free[2 + j], 1)
                    if t < TILES - 1:
                        dve.wait_ge(st_hi_s, here.nth(t + 2, 4, 16))
                        rest(st_lo[:], state[:], st_hi[:]).then_inc(st_lo_s, 1)

                def gate_o(c):
                    dve.wait_ge(turn_full, here.turned(T_HEAD + T_OT + c))
                    if c >= 2:
                        dve.wait_ge(yb_lo_s, here.nth(c - 1, 4, 16))
                    nc.vector.tensor_tensor(pair[:, c % 2, :], turn[c % 2][:], gate[:, c, :], ALU.mult)\
                        .then_inc(turn_free[c % 2], 1)

                def split_yb(c):
                    dve.wait_ge(yb_hi_s, here.nth(c + 1, 4, 16))
                    rest(yb_lo[:, c, :], pair[:, c % 2, :], yb_hi[:, c, :]).then_inc(yb_lo_s, 1)

                split_w(here, U_HEAD + U_F)
                gate_o(0)
                gate_o(1)
                split_yb(0)
                split_yb(1)
                split_w(here, U_HEAD + U_F + 1)
                gate_o(2)
                gate_o(3)
                split_yb(2)
                split_yb(3)
                order = half * ORDER_HALF + h * 10 + 10
                if not closing:
                    dve.wait_ge(yb_lo_s, here.nth(VT, 4, 16))
                    for part in range(2):
                        rotate(here, part, J_HEAD + J_F + 1, order, here.nth(3, 2, 2 * HEADS), 0)
                split_w(here, U_HEAD + U_F + 2)
                split_w(here, U_HEAD + U_F + 3)
                dve.wait_ge(acc_zero, half + 1)
                for i in range(4):
                    split_w(here, U_HEAD + U_WB + i)
                    for d in range(2):
                        if d:
                            dve.wait_ge(unit_done, here.used(U_HEAD + U_WB + i))
                        else:
                            dve.wait_ge(wb_first, here.nth(i + 1, 4, 16))
                        acc = y_acc[:, 2 * i + d, :]
                        nc.vector.tensor_tensor(acc, acc, proj[d][:], ALU.add).then_inc(proj_free[d], 1)
                        if i < 2 and d == 0 and not closing:
                            rotate(here, i, J_HEAD + J_F + 3, order + 5, here.nth(4, 2, 2 * HEADS), 2)

            for s, n in ((proj_free[0], 1), (proj_free[1], 1), (turn_free[0], 1), (turn_free[1], 1),
                         *((f, 1) for f in wide_free), (rope_done, 1), (pooled, 1)):
                dve.sem_inc(s, n)
            nc.vector.memset(state_all[:], 0.0).then_inc(zeroed, 1)
            nc.vector.memset(history[:], 0.0).then_inc(zeroed, 1)
            def make_h(here, t):
                for r in range(2):
                    dve.wait_ge(turn_full, here.turned(2 * t + r))
                    if t:
                        dve.wait_ge(h_lo_s, here.nth(2 * t + r - 1, 0, 2 * TILES))
                    nc.vector.tensor_tensor(
                        h_f[:, r, :].rearrange("p (k s) -> p k s", k=4),
                        turn[r][:].rearrange("p (k s) -> p k s", k=4),
                        gain_in[:, 4 * r:4 * r + 4].rearrange("p (k a) -> p k a", a=1).to_broadcast([P, 4, P]),
                        ALU.mult).then_inc(turn_free[r], 1)
                for r in range(2):
                    dve.wait_ge(h_hi_s, here.nth(2 * t + r + 1, 0, 2 * TILES))
                    rest(hT_lo[:, 4 * r:4 * r + 4, t * P:(t + 1) * P],
                         h_f[:, r, :].rearrange("p (k s) -> p k s", k=4),
                         hT_hi[:, 4 * r:4 * r + 4, t * P:(t + 1) * P]).then_inc(h_lo_s, 1)

            def first_split(u):
                dve.wait_ge(w_hi_s, u + 1)
                rest(w_lo[:, u, :], w_raw[:, u, :], w_hi[:, u, :]).then_inc(w_lo_s, 1)

            dve.wait_ge(first_consts_in, 16 * FIRST_CONSTS)
            for t in range(TILES):
                make_h(Place(0), t)
                if t:
                    first_split(t - 1)
            dve.wait_ge(zeroed, 2)
            dve.wait_ge(consts_in, 16 * CONSTS)
            with dve.Fori(0, HALVES) as half:
                here = Place(half)
                order = half * ORDER_HALF
                dve.wait_ge(trig_in, half * 16 + 16)
                for i in range(4):
                    split_w(here, U_KQ + i)
                    if i % 2:
                        for part in range(2):
                            rotate(here, part, J_KQ + i, order + i // 2 * 5, here.nth(1 + i // 2, 0, 2 * HEADS), i - 1)
                with dve.Fori(0, HEADS - 1) as h:
                    head(half, h, False)
                head(half, HEADS - 1, True)
                here = Place(half)
                for i in range(2):
                    dve.wait_ge(proj_free[i], here.proj_read(J_GB - 2 + i))
                nc.vector.tensor_tensor(y_acc[:, 0:4, :], y_acc[:, 0:4, :], kq[:], ALU.mult).then_inc(dve_order, 1)
                for i in range(4):
                    split_w(here, U_GB + i)
                    dve.wait_ge(proj_free[i % 2], here.proj_read(J_GB + i))
                    nc.vector.tensor_tensor(y_acc[:, 4 + i, :], y_acc[:, 4 + i, :], sig[:], ALU.mult)\
                        .then_inc(sig_used, 1)
                with dve.Fori(0, GROUPS) as g:
                    here = at_group(half, g)
                    consts = half * GROUPS + g
                    for j in range(2):
                        order = half * ORDER_HALF + g * 16 + (ORDER_POOL + 1 + 8 * j)
                        split_w(here, U_POOL + j)
                        dve.wait_ge(proj_free[j], here.proj_read(J_POOL + j))
                        past = history[:, g, j * HIST:(j + 1) * HIST]
                        nc.vector.tensor_copy(a_in[:, j, 0:HIST], past).then_inc(dve_order, 1)
                        src = a_in
                        for k in range(4):
                            dst = (pa, pb)[k % 2]
                            lo = 2 ** (k + 1) - 1
                            dve.wait_ge(dve_order, order + (k + 1))
                            nc.vector.scalar_tensor_tensor(
                                out=dst[:, j, lo:], in0=src[:, j, lo - 2 ** k:row - 2 ** k],
                                scalar=pool_k[:, consts, k:k + 1], in1=src[:, j, lo:], op0=ALU.mult, op1=ALU.add)\
                                .then_inc(dve_order, 1)
                            src = dst
                        dve.wait_ge(dve_order, order + 5)
                        nc.vector.tensor_tensor(tab_tmp[:], src[:, j, HIST:2 * HIST],
                                                pool_k[:, consts, 5:5 + HIST], ALU.mult).then_inc(dve_order, 1)
                        nc.vector.scalar_tensor_tensor(
                            out=po_f[:, j, HIST:], in0=src[:, j, 2 * HIST:], scalar=pool_k[:, consts, 4:5],
                            in1=a_in[:, j, 2 * HIST:], op0=ALU.mult, op1=ALU.subtract).then_inc(dve_order, 1)
                        nc.vector.tensor_copy(past, a_in[:, j, TOK:]).then_inc(dve_order, 1)
                        dve.wait_ge(dve_order, order + 8)
                        nc.vector.tensor_tensor(po_f[:, j, 0:HIST], tab_tmp[:], a_in[:, j, HIST:2 * HIST],
                                                ALU.subtract).then_inc(pooled, 1)
                        dve.wait_ge(pooled, here.nth(2 + j, 2, 2 * GROUPS))
                    split_w(here, U_POOL + 2)
                    dve.wait_ge(wp_hi_s, here.nth(1, 1, GROUPS))
                    rest(wp_lo[:], wp_raw[:, g, :], wp_hi[:]).then_inc(wp_lo_s, 1)
                    for i in range(2):
                        dve.wait_ge(a_sig_s, here.nth(i + 1, 2, 2 * GROUPS))
                        nc.vector.tensor_tensor(a_gate[:, i, :], proj[i][:], a_sig[:, i, :], ALU.mult)\
                            .then_inc(proj_free[i], 1)
                        dve.wait_ge(po_hi_s, here.nth(i + 1, 2, 2 * GROUPS))
                        rest(po_lo[:, i, :], po_f[:, i, :], po_hi[:, i, :]).then_inc(po_lo_s, 1)
                        if i == 0:
                            split_w(here, U_POOL + 3)
                    for j in range(2):
                        dve.wait_ge(mix_done, here.nth(j + 1, 2, 2 * GROUPS))
                        nc.vector.scalar_tensor_tensor(
                            out=ya_f[:, j, :], in0=proj[j][:], scalar=scale_k[:, bass.ds(g * 2 + j, 1)],
                            in1=a_gate[:, j, :], op0=ALU.mult, op1=ALU.mult).then_inc(proj_free[j], 1)
                    for j in range(2):
                        dve.wait_ge(ya_hi_s, here.nth(j + 1, 2, 2 * GROUPS))
                        rest(ya_lo[:, g * 2 + j, :], ya_f[:, j, :], ya_hi[:, g * 2 + j, :]).then_inc(ya_lo_s, 1)
                    dve.wait_ge(ya_lo_s, here.nth(2, 2, KT))
                with dve.Fori(0, KT // 2) as i:
                    here = at_merge(half, i)
                    for d in range(2):
                        for n in range(2):
                            split_w(here, U_MERGE + 2 * d + n)
                        if d == 0:
                            dve.wait_ge(sig_used, half * 4 + 4)
                            dve.wait_ge(dve_order, half * ORDER_HALF + ORDER_HALF)
                        dve.wait_ge(proj_free[0], here.proj_read(J_MERGE + 2 * d))
                        dve.wait_ge(unit_done, here.used(U_MERGE + 2 * d + 1))
                        nc.vector.tensor_tensor(m_a, proj[1][:], m_sig[:], ALU.mult).then_inc(proj_free[1], 1)
                        dve.wait_ge(proj_free[1], here.proj_read(J_MERGE + 2 * d + 1))
                        nc.vector.tensor_tensor(m_f, m_a, y_acc[:, i * 2 + d, :], ALU.add).then_inc(m_sum, 1)
                        dve.wait_ge(m_hi_s, here.nth(d + 1, 2, KT))
                        rest(m_lo[:, i * 2 + d, :], m_f, m_hi[:, i * 2 + d, :]).then_inc(m_lo_s, 1)
                        dve.wait_ge(m_lo_s, here.nth(d + 1, 2, KT))
                here, after = Place(half), Place(half + 1)

                def residual(e, t):
                    if t < TILES - 1:
                        dve.wait_ge(out_full, here.nth(e * (TILES - 1) + t + 1, 0, 2 * (TILES - 1)))
                    else:
                        dve.wait_ge(unit_done, here.used(U_OUT + 4 * e + 3))
                    cols = slice(e * 512, (e + 1) * 512)
                    nc.vector.tensor_tensor(y[:, t, cols], y[:, t, cols], wide[t][:], ALU.add).then_inc(wide_free[t], 1)

                def normalise(t):
                    dve.wait_ge(y_rstd, here.nth(t + 1, 0, TILES))
                    nc.vector.scalar_tensor_tensor(out=y[:, t, :], in0=y[:, t, :], scalar=y_rs[:, t:t + 1],
                                                   in1=gain_out[:], op0=ALU.mult, op1=ALU.mult).then_inc(y_ready, 1)

                split_w(here, U_OUT)
                dve.wait_ge(y_in, half * (16 * (TILES + 1)) + 16 * (TILES + 1))
                residual(0, 0)
                residual(0, 1)
                make_h(after, 0)
                residual(0, 2)
                make_h(after, 1)
                for u in range(1, 4):
                    split_w(here, U_OUT + u)
                residual(0, 3)
                split_w(here, U_OUT + 4)
                residual(1, 0)
                residual(1, 1)
                make_h(after, 2)
                normalise(0)
                residual(1, 2)
                make_h(after, 3)
                normalise(1)
                for u in range(5, 8):
                    split_w(here, U_OUT + u)
                residual(1, 3)
                normalise(2)
                normalise(3)


def weight_units(w_in, w_a, w_b, w_o):
    offs = np.cumsum((0, 1024, 1024, 1024, 1024, 2048, 2048, 1024, 1024))
    a_in, a_gate, q, k, v, r_gate, g_a, g_b = (w_in[:, offs[i]:offs[i + 1]] for i in range(8))

    def tiles(w, k, e, cols=P):
        rows = w[k[0] * P:k[1] * P, e:e + cols]
        return rows.reshape(k[1] - k[0], P, cols).transpose(1, 0, 2).reshape(P, -1)

    def kq_units(h):
        return [tiles(w, (0, KT), h * DK + j * P) for w in (k, q) for j in range(2)]

    units = kq_units(0)
    for h in range(HEADS):
        units += [tiles(v, (2 * u, 2 * u + 2), h * DV, DV) for u in range(4)]
        units += [tiles(r_gate, (0, KT), h * DV + c * P) for c in range(VT)]
        units += kq_units(h + 1) if h < HEADS - 1 else [tiles(g_b, (0, KT), i * P) for i in range(4)]
        units += [tiles(w_b, (h * VT, (h + 1) * VT), i * 2 * P, 2 * P) for i in range(4)]
    units += [tiles(g_b, (0, KT), (4 + i) * P) for i in range(4)]
    for g in range(GROUPS):
        units += [tiles(w, (0, KT), g * GROUP + j * P) for w in (a_in, a_gate) for j in range(2)]
    for d in range(KT):
        units += [tiles(g_a, (0, KT), d * P), tiles(w_a, (0, KT), d * P)]
    for e in range(2):
        units += [tiles(w_o, (2 * u, 2 * u + 2), e * 512, 512) for u in range(4)]
    assert len(units) == UNITS
    return np.ascontiguousarray(np.stack(units))


def shape_constants():
    half = DK // 2
    inv_freq = (1.0 / (np.float32(ROPE_BASE) ** (np.arange(half, dtype=np.float32) / np.float32(half)))).astype(np.float32)
    angle = np.arange(SEQ, dtype=np.float32)[None, :] * inv_freq[:, None]
    trig = np.stack([np.cos(angle.astype(np.float64)), np.sin(angle.astype(np.float64))], 1)
    trig = trig.reshape(P, 2, HALVES, TOK).transpose(2, 0, 1, 3)

    head = np.zeros((P, HEADS, HC))
    i = np.arange(P)
    for h in range(HEADS):
        gamma = 1.0 - 2.0 ** (-5.0 - h)
        seen = (i[:, None] // CHUNK) <= (i[None, :] // CHUNK)
        head[:, h, 0:P] = seen * gamma ** (np.abs(i[:, None] - i[None, :]) - (i[None, :] + 1.0)) * DK ** -0.5
        head[:, h, P] = gamma ** (P - 1.0 - i) * DK ** -0.5
        head[:, h, P + 1] = EPS / gamma ** (2.0 * (i + 1))
        head[:, h, P + 2] = gamma ** P

    pool = np.zeros((HALVES, GROUPS, PCOLS))
    for s in range(HALVES):
        for g, w in enumerate(WINDOWS):
            pool[s, g, 0:4] = [2 ** k < w for k in range(4)]
            pool[s, g, 4] = 1.0 / w
            pool[s, g, 5:] = 1.0 / np.minimum(s * TOK + np.arange(HIST) + 1, w)
    pool = np.broadcast_to(pool.reshape(1, HALVES * GROUPS, PCOLS), (P, HALVES * GROUPS, PCOLS))
    return [np.ascontiguousarray(a.astype(np.float32)) for a in (np.eye(P), trig, head, pool)]


def kernel(**inputs):
    import concourse.bacc as bacc
    from concourse.bass_utils import run_bass_kernel_spmd

    a = {n: np.asarray(v) for n, v in inputs.items()}
    ident, trig, head, pool = shape_constants()
    arrays = {
        "wstream": weight_units(a["w_in"], a["w_a"], a["w_b"], a["w_o"]),
        "x": a["x"],
        "norm_in": np.ascontiguousarray(a["norm_in"].reshape(KT, P).T),
        "w_pool": np.ascontiguousarray(a["w_pool"].reshape(GROUPS, 2, P, GROUP).transpose(2, 0, 1, 3)
                                       .reshape(P, GROUPS, 2 * GROUP)),
        "pool_scale": np.ascontiguousarray(a["pool_scale"].reshape(KT, P).T),
        "norm_out": np.ascontiguousarray(np.broadcast_to(a["norm_out"], (P, D_MODEL))),
        "ident": ident, "trig": trig, "head": head, "pool": pool,
    }
    nc = bacc.Bacc("TRN2", target_bir_lowering=False, num_devices=1)
    args = [nc.dram_tensor(f"in_{n}", v.shape, F32, kind="ExternalInput").ap() for n, v in arrays.items()]
    out = nc.dram_tensor("out", (1, SEQ, D_MODEL), F32, kind="ExternalOutput").ap()
    build(nc, *args, out)
    r = run_bass_kernel_spmd(nc, [{f"in_{n}": v for n, v in arrays.items()}], core_ids=[0])
    return r.results[0]["out"]
```

```python
from contextlib import ExitStack

import numpy as np
import concourse.bass as bass
from concourse import mybir

F32 = mybir.dt.float32
F32R = mybir.dt.float32r
ACT = mybir.ActivationFunctionType
ALU = mybir.AluOpType

P = 128
D_MODEL, SEQ = 1024, 1024
HALVES = 2
TOK = SEQ // HALVES
TILES = TOK // P
KT = D_MODEL // P
HEADS, DK, DV = 4, 256, 512
VT = DV // P
CHUNK = 64
WINDOWS = (2, 4, 8, 16)
GROUPS, GROUP = 4, 256
HIST = 16
EPS = 1e-6
ROPE_BASE = 10000.0
RING = 4

U_KQ = 0
U_HEAD = 4
U_V, U_G, U_F, U_WB = 0, 4, 8, 12
U_POOL = U_HEAD + 16 * HEADS
U_GB = U_POOL + 4 * GROUPS
U_MERGE = U_GB + 4
U_OUT = U_MERGE + 2 * KT
UNITS = U_OUT + 8

J_KQ = 0
J_HEAD = 4
J_G, J_F, J_WB = 0, 4, 8
J_POOL = J_HEAD + 16 * HEADS
J_GB = J_POOL + 4 * GROUPS
J_MERGE = J_GB + 4
PROJ_JOBS = J_MERGE + 2 * KT

T_HEAD = 2
T_OT = 2 * TILES
TURN_HEAD = T_OT + VT
T_MIX = T_HEAD + TURN_HEAD * HEADS
TURN_JOBS = T_MIX + 2 * GROUPS

STORES = (*((t, slice(0, D_MODEL)) for t in range(TILES - 1)),
          (TILES - 1, slice(0, D_MODEL // 2)), (TILES - 1, slice(D_MODEL // 2, D_MODEL)))
X_SUMS = 1 + KT

WIDE_HEAD = (3, 3, 5, 5)
WIDE_HALF = tuple(HEADS * n + 2 for n in WIDE_HEAD)

ORDER_POOL = 10 * HEADS
ORDER_HALF = ORDER_POOL + 1 + 8 * GROUPS
CONSTS = 3

X_LOADS = KT // 2

HC = P + 3
PCOLS = 5 + HIST


def build(nc, wstream, x, x_turned, norm_in, w_pool, pool_scale, norm_out, ident_c, trig_c, head_c, pool_c, out):
    with ExitStack() as ctx:
        def sem(name):
            return ctx.enter_context(nc.semaphore(name))

        top = [(nc.sbuf_base + 31) // 32 * 32]

        def at(name, shape, dt, offset):
            return nc.alloc_sbuf_tensor_at(name, [P, *shape], dt, offset=offset)

        def keep(name, shape, dt=F32):
            t = at(name, shape, dt, top[0])
            top[0] += (4 * int(np.prod(shape)) + 31) // 32 * 32
            return t

        hT_hi, hT_lo = keep("hT_hi", [KT, TOK], F32R), keep("hT_lo", [KT, TOK], F32R)
        w_hi, w_lo = keep("w_hi", [RING, 1024], F32R), keep("w_lo", [RING, 1024], F32R)
        w_raw = keep("w_raw", [RING, 1024])
        state_all = keep("state_all", [HEADS, 2 * DV])
        y_acc = keep("y_acc", [KT, TOK])
        ident = keep("ident", [P])
        trig = keep("trig", [2, TOK])
        head_k = keep("head_k", [HEADS, HC])
        pool_k = keep("pool_k", [HALVES * GROUPS, PCOLS])
        history = keep("history", [GROUPS, 2 * HIST])
        gain_in = keep("gain_in", [KT])
        scale_k = keep("scale_k", [KT])
        ssq, ms, rstd, minus_half, eps_k, eps_head, zeta, inv_dv, inv_dm = (keep(n, [1]) for n in (
            "ssq", "ms", "rstd", "minus_half", "eps_k", "eps_head", "zeta", "inv_dv", "inv_dm"))
        y_ssq, y_rs = keep("y_ssq", [TILES]), keep("y_rs", [TILES])
        mean_w, x_ms, x_rs = keep("mean_w", [1]), keep("x_ms", [TILES]), keep("x_rs", [TILES])
        ones, x_rs_row = keep("ones", [P]), keep("x_rs_row", [TOK])
        tab_tmp = keep("tab_tmp", [2, HIST])

        R, K = top[0], 1024
        v_hi, v_lo = at("v_hi", [TILES, DV], F32R, R), at("v_lo", [TILES, DV], F32R, R + 8 * K)
        yb_hi, yb_lo = at("yb_hi", [VT, TOK], F32R, R + 16 * K), at("yb_lo", [VT, TOK], F32R, R + 24 * K)
        kq = at("kq", [4, TOK], F32, R + 32 * K)
        gate = at("gate", [VT, TOK], F32, R + 40 * K)
        o_n = at("o_n", [TILES, DV], F32, R + 48 * K)
        st_hi, st_lo = at("st_hi", [2, DV], F32R, R + 56 * K), at("st_lo", [2, DV], F32R, R + 60 * K)
        state = at("state", [2, DV], F32, R + 64 * K)
        rope_in = at("rope_in", [2, TOK], F32, R + 68 * K)
        pair = at("pair", [2, TOK], F32, R + 72 * K)
        sig = at("sig", [TOK], F32, R + 76 * K)
        sc_f, sc_hi, sc_lo = (at(n, [P], d, R + 78 * K + i * 512) for i, (n, d) in enumerate(
            (("sc_f", F32), ("sc_hi", F32R), ("sc_lo", F32R))))
        kn_f, kn_hi, kn_lo, q_hi, q_lo = (at(n, [DK], d, R + 79 * K + 512 + i * K) for i, (n, d) in enumerate(
            (("kn_f", F32), ("kn_hi", F32R), ("kn_lo", F32R), ("q_hi", F32R), ("q_lo", F32R))))
        xT = at("xT", [KT, TOK], F32, R + 64 * K)
        squares = [at(f"squares{i}", [TOK], F32, R + (80, 62)[i] * K) for i in range(2)]
        sq_sum = at("sq_sum", [TOK], F32, R + 82 * K)
        x_diag = at("x_diag", [TILES, P], F32, R + 80 * K)
        ya_hi, ya_lo = at("ya_hi", [KT, TOK], F32R, R), at("ya_lo", [KT, TOK], F32R, R + 16 * K)
        row = HIST + TOK
        a_in, pa, pb = (at(n, [2, row], F32, R + 32 * K + i * 8 * row) for i, n in enumerate(("a_in", "pa", "pb")))
        po_f, po_hi, po_lo = (at(n, [2, TOK], d, R + 45 * K + 4 * K * i) for i, (n, d) in enumerate(
            (("po_f", F32), ("po_hi", F32R), ("po_lo", F32R))))
        wp_hi, wp_lo = at("wp_hi", [2 * GROUP], F32R, R + 57 * K), at("wp_lo", [2 * GROUP], F32R, R + 59 * K)
        wp_raw = at("wp_raw", [GROUPS, 2 * GROUP], F32, R + 64 * K)
        a_sig, a_gate, ya_f = (at(n, [2, TOK], F32, R + (72 + 4 * i) * K) for i, n in enumerate(
            ("a_sig", "a_gate", "ya_f")))
        gb_sig = pa[:, 0, 0:TOK]
        m_hi, m_lo = at("m_hi", [KT, TOK], F32R, R + 32 * K), at("m_lo", [KT, TOK], F32R, R + 48 * K)
        y = at("y", [TILES, D_MODEL], F32, R + 16 * K)
        gain_out = at("gain_out", [D_MODEL], F32, R)
        m_f, m_sig = trig[:, 0, :], trig[:, 1, :]
        out_junk = at("out_junk", [D_MODEL], F32, R + 8 * K)
        assert R + 84 * K + 512 <= nc.sbuf_usable_end, R

        proj = [ctx.enter_context(nc.psum_tensor(f"proj{i}", [P, 512], F32)) for i in range(2)]
        wide = [ctx.enter_context(nc.psum_tensor(f"wide{i}", [P, 512], F32)) for i in range(4)]
        turn = [ctx.enter_context(nc.psum_tensor(f"turn{i}", [P, 512], F32)) for i in range(2)]

        ident_in, consts_in = sem("ident_in"), sem("consts_in")
        raw_in = [sem(f"raw_in{i}") for i in range(RING)]
        x_in = [sem(f"x_in{i}") for i in range(X_LOADS)]
        trig_in, wp_in, y_in = sem("trig_in"), sem("wp_in"), sem("y_in")
        stored = sem("stored")
        unit_done = sem("unit_done")
        wb_first = sem("wb_first")
        turn_full = sem("turn_full")
        o_full, upd_full = sem("o_full"), sem("upd_full")
        out_full = sem("out_full")
        proj_free = [sem(f"proj_free{i}") for i in range(2)]
        turn_free = [sem(f"turn_free{i}") for i in range(2)]
        wide_free = [sem(f"wide_free{i}") for i in range(4)]
        w_hi_s, w_lo_s = sem("w_hi_ready"), sem("w_lo_ready")
        h_hi_s, h_lo_s = sem("h_hi_ready"), sem("h_lo_ready")
        v_hi_s, q_hi_s, q_lo_s = sem("v_hi_ready"), sem("q_hi_ready"), sem("q_lo_ready")
        sc_hi_s, sc_lo_s = sem("sc_hi_ready"), sem("sc_lo_ready")
        kn_hi_s, kn_lo_s = sem("kn_hi_ready"), sem("kn_lo_ready")
        st_hi_s, st_lo_s = sem("st_hi_ready"), sem("st_lo_ready")
        yb_hi_s, yb_lo_s = sem("yb_hi_ready"), sem("yb_lo_ready")
        po_hi_s, po_lo_s = sem("po_hi_ready"), sem("po_lo_ready")
        wp_hi_s, wp_lo_s = sem("wp_hi_ready"), sem("wp_lo_ready")
        ya_hi_s, ya_lo_s = sem("ya_hi_ready"), sem("ya_lo_ready")
        m_hi_s, m_lo_s = sem("m_hi_ready"), sem("m_lo_ready")
        x_sq, x_sum, x_rstd = sem("x_sq"), sem("x_sum"), sem("x_rstd")
        mean_ready, x_diag_s = sem("mean_ready"), sem("x_diag_ready")
        o_sq, o_rstd = sem("o_sq"), sem("o_rstd")
        y_sq, y_rstd, y_ready = sem("y_sq"), sem("y_rstd"), sem("y_ready")
        rope_done = sem("rope_done")
        trig_ready = sem("trig_ready")
        gate_sig, gate_done = sem("gate_sig"), sem("gate_done")
        a_sig_s, a_gate_done = sem("a_sig_ready"), sem("a_gate_done")
        gb_sig_s, sig_used, m_sig_s = sem("gb_sig_ready"), sem("sig_used"), sem("m_sig_ready")
        pooled = sem("pooled")
        m_sum = sem("m_sum")
        acc_zero = sem("acc_zero")
        dve_order, pool_order = sem("dve_order"), sem("pool_order")
        zeroed = sem("zeroed")
        zeta_ready = sem("zeta_ready")
        pe_seen, pool_seen = sem("pe_seen"), sem("pool_seen")

        x_t = x.rearrange("b (h t p) d -> (b h) t p d", h=HALVES, t=TILES)
        xT_t = x_turned.rearrange("h p (q k s) -> h q p k s", q=X_LOADS, k=2)
        out_t = out.rearrange("b (h t p) d -> (b h) t p d", h=HALVES, t=TILES)

        block = ctx.enter_context(nc.Block())

        class Place:

            def __init__(self, half, s=0, units=0, projs=0, turns=0):
                self.half, self.s, self.units, self.projs, self.turns = half, s, units, projs, turns

            def split(self, u):
                return self.half * UNITS + self.s * self.units + (u + 1)

            def used(self, u):
                return self.half * UNITS + self.s * self.units + (u + 2)

            def loaded(self, u):
                return self.half * (16 * UNITS // RING) + self.s * (16 * self.units // RING) + 16 * (u // RING + 1)

            def proj_open(self, j):
                return self.half * (PROJ_JOBS // 2) + self.s * (self.projs // 2) + (j // 2 + 1)

            def proj_read(self, j):
                return self.proj_open(j) + 1

            def turn_open(self, j):
                return self.half * (TURN_JOBS // 2) + self.s * (self.turns // 2) + (j // 2 + 1)

            def turn_read(self, j):
                return self.turn_open(j) + 1

            def turned(self, j):
                return self.half * TURN_JOBS + self.s * self.turns + (j + 1)

            def wide_open(self, b, n):
                return self.half * WIDE_HALF[b] + self.s * WIDE_HEAD[b] + (n + 1)

            def nth(self, n, per_step, per_half):
                return self.half * per_half + self.s * per_step + n

        def at_head(half, h):
            return Place(half, h, 16, 16, TURN_HEAD)

        def at_group(half, g):
            return Place(half, g, 4, 4, 2)

        def at_merge(half, i):
            return Place(half, i, 4, 4)

        def x_loaded(q, half):
            return half * 16 + (32 if q == 0 else 16)

        @block.sync
        def _(sp):
            def first_x(q):
                sp.dma_start(xT[:, 2 * q:2 * q + 2, :], xT_t[0, q]).then_inc(x_in[q], 16)

            def first_unit(r):
                sp.dma_start(w_raw[:, r, :], wstream[r]).then_inc(raw_in[r], 16)

            first_x(0)
            sp.dma_start(gain_in[:], norm_in).then_inc(x_in[0], 16)
            first_unit(0)
            first_unit(1)
            for q in range(1, X_LOADS):
                first_x(q)
            first_unit(2)
            sp.dma_start(ident[:], ident_c).then_inc(ident_in, 16)
            first_unit(3)
            sp.dma_start(trig[:], trig_c[0]).then_inc(trig_in, 16)
            sp.dma_start(head_k[:], head_c).then_inc(consts_in, 16)
            sp.dma_start(pool_k[:], pool_c).then_inc(consts_in, 16)
            sp.dma_start(scale_k[:], pool_scale).then_inc(consts_in, 16)

            def load_units(half, first, last):
                with sp.Fori(first // RING, last // RING) as q:
                    for r in range(RING):
                        sp.wait_ge(w_lo_s, half * UNITS + q * RING + (r + 1))
                        sp.dma_start(w_raw[:, r, :], wstream[q * RING + (RING + r)]).then_inc(raw_in[r], 16)

            with sp.Fori(0, HALVES) as half:
                here = Place(half)
                load_units(half, 0, U_POOL)
                sp.wait_ge(yb_lo_s, here.nth(HEADS * VT, 0, HEADS * VT))
                sp.dma_start(wp_raw[:], w_pool).then_inc(wp_in, 16)
                load_units(half, U_POOL, U_MERGE)
                sp.wait_ge(ya_lo_s, here.nth(KT, 0, KT))
                for q in range(X_LOADS):
                    sp.dma_start(xT[:, 2 * q:2 * q + 2, :], xT_t[HALVES - 1, q]).then_inc(x_in[q], 16)
                load_units(half, U_MERGE, U_OUT)
                sp.wait_ge(unit_done, here.used(U_OUT - 1))
                for t in range(TILES):
                    sp.dma_start(y[:, t, :], x_t[half, t]).then_inc(y_in, 16)
                sp.dma_start(gain_out[:], norm_out).then_inc(y_in, 16)
                load_units(half, U_OUT, UNITS - RING)
                for r in range(RING):
                    sp.wait_ge(w_lo_s, here.split(UNITS - RING + r))
                    sp.dma_start(w_raw[:, r, :], wstream[r]).then_inc(raw_in[r], 16)
                sp.wait_ge(m_lo_s, here.nth(KT, 0, KT))
                sp.dma_start(trig[:], trig_c[HALVES - 1]).then_inc(trig_in, 16)
                for i, (t, cols) in enumerate(STORES):
                    sp.wait_ge(y_ready, here.nth(i + 1, 0, len(STORES)))
                    sp.dma_start(out_t[half, t, :, cols], y[:, t, cols]).then_inc(stored, 16)
            sp.wait_ge(stored, 16 * len(STORES) * HALVES)
            for q in range(X_LOADS):
                sp.wait_ge(x_in[q], x_loaded(q, HALVES))
            sp.wait_ge(trig_in, 16 * (HALVES + 1))
            for r in range(RING):
                sp.wait_ge(raw_in[r], 16 * (HALVES * UNITS // RING + 1))

        @block.tensor
        def _(pe):
            def mm3(dst, a_hi, a_lo, b_hi, b_lo, first, last):
                nc.tensor.matmul(dst, a_hi, b_hi, start=first, stop=False)
                nc.tensor.matmul(dst, a_hi, b_lo, start=False, stop=False)
                return nc.tensor.matmul(dst, a_lo, b_hi, start=False, stop=last)

            def slot(u, k):
                s = u % RING
                return (w_hi[:, s, :].rearrange("p (k e) -> p k e", k=k),
                        w_lo[:, s, :].rearrange("p (k e) -> p k e", k=k))

            def project(here, u, j, b_hi, b_lo):
                pe.wait_ge(w_lo_s, here.split(u))
                pe.wait_ge(proj_free[j % 2], here.proj_open(j))
                wh, wl = slot(u, KT)
                for k in range(KT):
                    mm = mm3(proj[j % 2][:], wh[:, k, :], wl[:, k, :], b_hi[:, k, :], b_lo[:, k, :],
                             k == 0, k == KT - 1)
                mm.then_inc(unit_done, 1)

            def natural(here, u, n, a_hi, a_lo):
                pe.wait_ge(w_lo_s, here.split(u))
                wh, wl = slot(u, 2)
                for t in range(TILES):
                    cols = slice(t * P, (t + 1) * P)
                    for k in range(2):
                        mm = mm3(wide[t][:], a_hi[:, 2 * n + k, cols], a_lo[:, 2 * n + k, cols],
                                 wh[:, k, :], wl[:, k, :], n == 0 and k == 0, n == 3 and k == 1)
                mm.then_inc(unit_done, 1)

            def head(half, h):
                here = at_head(half, h)
                for b in range(4):
                    pe.wait_ge(wide_free[b], here.wide_open(b, 0))
                for u in range(4):
                    natural(here, U_HEAD + U_V + u, u, hT_hi, hT_lo)
                pe.wait_ge(rope_done, here.nth(3, 2, 2 * HEADS))
                for t in range(TILES):
                    cols = slice(t * P, (t + 1) * P)
                    pe.wait_ge(turn_free[0], here.turn_open(T_HEAD + 2 * t))
                    for j in range(2):
                        mm = nc.tensor.matmul(turn[0][:, 0:P], kq[:, j, cols], kq[:, 2 + j, cols],
                                              start=j == 0, stop=j == 1)
                    mm.then_inc(turn_full, 1)
                    pe.wait_ge(turn_free[1], here.turn_open(T_HEAD + 2 * t + 1))
                    for j in range(2):
                        mm = nc.tensor.transpose(turn[1][:, j * P:(j + 1) * P], kq[:, j, cols], ident[:])
                    mm.then_inc(turn_full, 1)
                    project(here, U_HEAD + U_G + t, J_HEAD + J_G + t, hT_hi, hT_lo)
                    o = wide[t % 2]
                    pe.wait_ge(wide_free[t % 2], here.wide_open(t % 2, 1 + t // 2))
                    pe.wait_ge(sc_lo_s, here.nth(t + 1, 4, 16))
                    mm3(o[:], sc_hi[:], sc_lo[:], v_hi[:, t, :], v_lo[:, t, :], True, False)
                    pe.wait_ge(q_lo_s, here.nth(t + 1, 4, 16))
                    pe.wait_ge(st_lo_s, here.nth(t + 1, 4, 16))
                    for j in range(2):
                        mm = mm3(o[:], q_hi[:, j * P:(j + 1) * P], q_lo[:, j * P:(j + 1) * P],
                                 st_hi[:, j, :], st_lo[:, j, :], False, j == 1)
                    mm.then_inc(o_full, 1)
                    pe.wait_ge(kn_lo_s, here.nth(t + 1, 4, 16))
                    for j in range(2):
                        pe.wait_ge(wide_free[2 + j], here.wide_open(2 + j, 1 + t))
                        mm = mm3(wide[2 + j][:], kn_hi[:, j * P:(j + 1) * P], kn_lo[:, j * P:(j + 1) * P],
                                 v_hi[:, t, :], v_lo[:, t, :], True, True)
                    mm.then_inc(upd_full, 1)

                def filler(i):
                    project(here, U_HEAD + U_F + i, J_HEAD + J_F + i, hT_hi, hT_lo)

                def turn_o(c):
                    pe.wait_ge(turn_free[c % 2], here.turn_open(T_HEAD + T_OT + c))
                    for t in range(TILES):
                        mm = nc.tensor.transpose(turn[c % 2][:, t * P:(t + 1) * P],
                                                 o_n[:, t, c * P:(c + 1) * P], ident[:])
                    mm.then_inc(turn_full, 1)

                filler(0)
                for b in range(2):
                    pe.wait_ge(wide_free[b], here.wide_open(b, 3))
                turn_o(0)
                turn_o(1)
                filler(1)
                turn_o(2)
                turn_o(3)
                filler(2)
                filler(3)
                pe.wait_ge(yb_lo_s, here.nth(VT, VT, HEADS * VT))
                for i in range(4):
                    u = U_HEAD + U_WB + i
                    pe.wait_ge(w_lo_s, here.split(u))
                    wh, wl = slot(u, VT)
                    for d in range(2):
                        pe.wait_ge(proj_free[d], here.proj_open(J_HEAD + J_WB + 2 * i + d))
                        for k in range(VT):
                            mm = mm3(proj[d][:], wh[:, k, d * P:(d + 1) * P], wl[:, k, d * P:(d + 1) * P],
                                     yb_hi[:, k, :], yb_lo[:, k, :], k == 0, k == VT - 1)
                        mm.then_inc(unit_done if d else wb_first, 1)

            def mean_square(here):
                pe.wait_ge(x_sum, here.nth(X_SUMS, 0, X_SUMS))
                pe.wait_ge(turn_free[0], here.turn_open(0))
                for t in range(TILES):
                    mm = nc.tensor.matmul(turn[0][:, t:t + 1], sq_sum[:, t * P:(t + 1) * P], mean_w[:],
                                          start=True, stop=True)
                mm.then_inc(turn_full, 1)

            def spread(here):
                pe.wait_ge(x_diag_s, here.nth(1, 0, 1))
                pe.wait_ge(turn_free[1], here.turn_open(1))
                nc.tensor.matmul(turn[1][:], ones[:], x_diag[:].rearrange("p t s -> p (t s)"),
                                 start=True, stop=True).then_inc(turn_full, 1)

            pe.sem_inc(unit_done, 1)
            pe.wait_ge(mean_ready, 2)
            pe.sem_inc(pe_seen, 1)
            with pe.Fori(0, HALVES) as half:
                here = Place(half)
                for q in range(X_LOADS):
                    for j in range(2):
                        if q == 0:
                            pe.wait_ge(w_lo_s, here.split(U_KQ + j))
                            pe.wait_ge(proj_free[j], here.proj_open(J_KQ + j))
                        wh, wl = slot(U_KQ + j, KT)
                        for k in (2 * q, 2 * q + 1):
                            if j == 0:
                                pe.wait_ge(h_lo_s, here.nth(k + 1, 0, KT))
                            mm = mm3(proj[j][:], wh[:, k, :], wl[:, k, :], hT_hi[:, k, :], hT_lo[:, k, :],
                                     k == 0, k == KT - 1)
                        if k == KT - 1:
                            mm.then_inc(unit_done, 1)
                mean_square(here)
                project(here, U_KQ + 2, J_KQ + 2, hT_hi, hT_lo)
                spread(here)
                project(here, U_KQ + 3, J_KQ + 3, hT_hi, hT_lo)
                with pe.Fori(0, HEADS - 1) as h:
                    head(half, h)
                head(half, HEADS - 1)
                for i in range(2):
                    project(here, U_POOL + i, J_POOL + i, hT_hi, hT_lo)
                with pe.Fori(0, GROUPS) as g:
                    here = at_group(half, g)
                    for i in range(2, 6):
                        project(here, U_POOL + i, J_POOL + i, hT_hi, hT_lo)
                    pe.wait_ge(wp_lo_s, here.nth(1, 1, GROUPS))
                    pe.wait_ge(po_lo_s, here.nth(2, 2, 2 * GROUPS))
                    for j in range(2):
                        pe.wait_ge(turn_free[j], here.turn_open(T_MIX + j))
                        for k in range(2):
                            e = k * GROUP + j * P
                            mm = mm3(turn[j][:], wp_hi[:, e:e + P], wp_lo[:, e:e + P],
                                     po_hi[:, k, :], po_lo[:, k, :], k == 0, k == 1)
                        mm.then_inc(turn_full, 1)
                here = Place(half)
                for i in (2, 3):
                    project(here, U_GB + i, J_GB + i, hT_hi, hT_lo)
                with pe.Fori(0, KT // 2) as i:
                    here = at_merge(half, i)
                    for d in range(2):
                        project(here, U_MERGE + 2 * d, J_MERGE + 2 * d, hT_hi, hT_lo)
                        pe.wait_ge(ya_lo_s, Place(half).nth(KT, 0, KT))
                        project(here, U_MERGE + 2 * d + 1, J_MERGE + 2 * d + 1, ya_hi, ya_lo)
                here = Place(half)
                for e in range(2):
                    for t in range(TILES):
                        cols = slice(t * P, (t + 1) * P)
                        pe.wait_ge(wide_free[t], half * WIDE_HALF[t] + (WIDE_HALF[t] - 1 + e))
                        for n in range(4):
                            u = U_OUT + 4 * e + n
                            if t == 0:
                                pe.wait_ge(w_lo_s, here.split(u))
                                if e == 0:
                                    pe.wait_ge(m_lo_s, here.nth(2 * n + 2, 0, KT))
                            wh, wl = slot(u, 2)
                            for k in range(2):
                                mm = mm3(wide[t][:], m_hi[:, 2 * n + k, cols], m_lo[:, 2 * n + k, cols],
                                         wh[:, k, :], wl[:, k, :], n == 0 and k == 0, n == 3 and k == 1)
                            if t == TILES - 1:
                                mm.then_inc(unit_done, 1)
                        if t < TILES - 1:
                            mm.then_inc(out_full, 1)

        @block.scalar
        def _(act):
            def copy(dst, src):
                return nc.scalar.activation(dst, src, ACT.Copy)

            def split_w(here, u):
                s = (u + 3) % RING
                act.wait_ge(raw_in[s], here.loaded(u + 3))
                act.wait_ge(unit_done, here.used(u - 1))
                copy(w_hi[:, s, :], w_raw[:, s, :]).then_inc(w_hi_s, 1)

            def rope_copy(here, u, j, rope):
                act.wait_ge(unit_done, here.used(u))
                if j % 2 == 0:
                    act.wait_ge(rope_done, rope)
                copy(rope_in[:, j % 2, :], proj[j % 2][:]).then_inc(proj_free[j % 2], 1)

            def head(half, h, closing):
                here = at_head(half, h)
                copy(zeta[:], head_k[:, h, P:P + 1]).then_inc(zeta_ready, 1)
                for u in range(4):
                    split_w(here, U_HEAD + U_V + u)
                    if u == 1:
                        copy(st_hi[:].rearrange("p j e -> p (j e)"), state_all[:, h, :]).then_inc(st_hi_s, 1)
                act.wait_ge(unit_done, here.used(U_HEAD + U_V + 3))
                for t in range(TILES):
                    nc.scalar.activation(v_hi[:, t, :], wide[t][:], ACT.Copy,
                                         scale=x_rs[:, t:t + 1]).then_inc(v_hi_s, 1)
                act.wait_ge(zeta_ready, here.nth(1, 1, HEADS))
                act.wait_ge(rope_done, here.nth(3, 2, 2 * HEADS))
                for t in range(TILES):
                    cols = slice(t * P, (t + 1) * P)
                    if t:
                        act.wait_ge(o_full, here.nth(t, 4, 16))
                        act.wait_ge(q_lo_s, here.nth(t, 4, 16))
                    copy(q_hi[:].rearrange("p (j s) -> p j s", j=2), kq[:, 2:4, cols]).then_inc(q_hi_s, 1)
                    act.wait_ge(turn_free[0], here.turn_read(T_HEAD + 2 * t))
                    copy(sc_hi[:], sc_f[:]).then_inc(sc_hi_s, 1)
                    act.wait_ge(turn_full, here.turned(T_HEAD + 2 * t + 1))
                    if t:
                        act.wait_ge(upd_full, here.nth(t, 4, 16))
                        act.wait_ge(kn_lo_s, here.nth(t, 4, 16))
                    nc.scalar.activation(kn_f[:], turn[1][:, 0:DK], ACT.Copy,
                                         scale=zeta[:]).then_inc(turn_free[1], 1)
                    act.wait_ge(turn_free[1], here.turn_read(T_HEAD + 2 * t + 1))
                    copy(kn_hi[:], kn_f[:]).then_inc(kn_hi_s, 1)
                    split_w(here, U_HEAD + U_G + t)
                    act.wait_ge(proj_free[t % 2], here.proj_read(J_HEAD + J_G + t))
                    if t:
                        act.wait_ge(gate_done, here.nth(t, 4, 16))
                    nc.scalar.activation(sig[:], gate[:, t, :], ACT.Sigmoid).then_inc(gate_sig, 1)
                    act.wait_ge(o_full, here.nth(t + 1, 4, 16))
                    nc.scalar.activation(o_n[:, t, :], wide[t % 2][:], ACT.Square, accum_out=ssq[:]).then_inc(o_sq, 1)
                    if t < TILES - 1:
                        for j in range(2):
                            act.wait_ge(wide_free[2 + j], here.wide_open(2 + j, 2 + t))
                        copy(st_hi[:], state[:]).then_inc(st_hi_s, 1)
                    act.wait_ge(o_rstd, here.nth(t + 1, 4, 16))
                    nc.scalar.activation(o_n[:, t, :], wide[t % 2][:], ACT.Copy,
                                         scale=rstd[:]).then_inc(wide_free[t % 2], 1)

                def filled(i):
                    u, j = U_HEAD + U_F + i, J_HEAD + J_F + i
                    if closing:
                        act.wait_ge(proj_free[i % 2], here.proj_read(j))
                        nc.scalar.activation(kq[:, i, :], kq[:, i, :], ACT.Sigmoid).then_inc(gb_sig_s, 1)
                    else:
                        rope_copy(here, u, j, here.nth(3 + i // 2, 2, 2 * HEADS))

                def split_yb(c):
                    act.wait_ge(turn_free[c % 2], here.turn_read(T_HEAD + T_OT + c))
                    copy(yb_hi[:, c, :], pair[:, c % 2, :]).then_inc(yb_hi_s, 1)

                split_w(here, U_HEAD + U_F)
                filled(0)
                split_yb(0)
                split_yb(1)
                split_w(here, U_HEAD + U_F + 1)
                filled(1)
                split_yb(2)
                split_yb(3)
                for i in (2, 3):
                    split_w(here, U_HEAD + U_F + i)
                    filled(i)
                for i in range(4):
                    split_w(here, U_HEAD + U_WB + i)

            def x_square(here, i, d):
                act.wait_ge(x_sum, here.half * X_SUMS + 2 * i + 1)
                nc.scalar.activation(squares[d][:], xT[:, 2 * i + d, :], ACT.Square).then_inc(x_sq, 1)

            def x_mean(here):
                act.wait_ge(turn_full, here.turned(0))
                nc.scalar.activation(x_ms[:], turn[0][:, 0:TILES], ACT.Identity, bias=eps_k[:])\
                    .then_inc(turn_free[0], 1)

            def x_spread(here):
                act.wait_ge(turn_full, here.turned(1))
                copy(x_rs_row[:], turn[1][:]).then_inc(turn_free[1], 1)

            def split_h(here, k):
                nc.scalar.activation(hT_hi[:, k, :], xT[:, k, :], ACT.Copy, scale=gain_in[:, k:k + 1])\
                    .then_inc(h_hi_s, 1)

            def first_split(u):
                act.wait_ge(raw_in[u], 16)
                copy(w_hi[:, u, :], w_raw[:, u, :]).then_inc(w_hi_s, 1)

            def y_square(here, t):
                act.wait_ge(wide_free[t], here.wide_open(t, WIDE_HALF[t]))
                act.wait_ge(y_sq, here.nth(t + 1, 0, TILES))
                nc.scalar.activation(out_junk[:], y[:, t, :], ACT.Square, accum_out=y_ssq[:, t:t + 1])\
                    .then_inc(y_sq, 1)

            act.sem_inc(y_sq, 1)
            for i in range(X_LOADS):
                act.wait_ge(x_in[i], x_loaded(i, 0))
                split_h(Place(0), 2 * i)
                split_h(Place(0), 2 * i + 1)
                if i == 0:
                    first_split(0)
                    first_split(1)
                for d in range(2):
                    x_square(Place(0), i, d)
            first_split(2)
            act.wait_ge(pool_order, 4)
            act.wait_ge(consts_in, 16 * CONSTS)
            with act.Fori(0, HALVES) as half:
                here = Place(half)
                split_w(here, U_KQ)
                for i in range(2):
                    rope_copy(here, U_KQ + i, J_KQ + i, here.nth(1, 2, 2 * HEADS))
                x_mean(here)
                split_w(here, U_KQ + 1)
                split_w(here, U_KQ + 2)
                x_spread(here)
                split_w(here, U_KQ + 3)
                for i in (2, 3):
                    rope_copy(here, U_KQ + i, J_KQ + i, here.nth(2, 2, 2 * HEADS))
                with act.Fori(0, HEADS - 1) as h:
                    head(half, h, False)
                head(half, HEADS - 1, True)

                def take_g_b(here, i):
                    split_w(here, U_GB + i)
                    act.wait_ge(proj_free[i % 2], here.proj_read(J_GB + i))
                    nc.scalar.activation(gb_sig, gb_sig, ACT.Sigmoid).then_inc(gb_sig_s, 1)

                def group(g, closing):
                    here = at_group(half, g)
                    for i in range(2):
                        split_w(here, U_POOL + 2 + i)
                        act.wait_ge(proj_free[i], here.proj_read(J_POOL + 2 + i))
                        nc.scalar.activation(a_sig[:, i, :], a_gate[:, i, :], ACT.Sigmoid).then_inc(a_sig_s, 1)
                        if i == 0:
                            act.wait_ge(wp_in, half * 16 + 16)
                            copy(wp_hi[:], wp_raw[:, g, :]).then_inc(wp_hi_s, 1)
                        act.wait_ge(pooled, here.nth(2, 1, GROUPS))
                        copy(po_hi[:, i, :], po_f[:, i, :]).then_inc(po_hi_s, 1)
                    for i in range(2):
                        if closing:
                            take_g_b(Place(half), i)
                        else:
                            split_w(here, U_POOL + 4 + i)
                    for j in range(2):
                        act.wait_ge(turn_free[j], here.turn_read(T_MIX + j))
                        copy(ya_hi[:, g * 2 + j, :], ya_f[:, j, :]).then_inc(ya_hi_s, 1)

                for i in range(2):
                    split_w(here, U_POOL + i)
                with act.Fori(0, GROUPS - 1) as g:
                    group(g, False)
                group(GROUPS - 1, True)
                for i in (2, 3):
                    take_g_b(here, i)
                split_w(here, U_MERGE)
                for q in range(X_LOADS):
                    act.wait_ge(x_in[q], x_loaded(q, half + 1))
                with act.Fori(0, KT // 2) as i:
                    here = at_merge(half, i)
                    for d in range(2):
                        split_w(here, U_MERGE + 2 * d + 1)
                        act.wait_ge(proj_free[0], here.proj_read(J_MERGE + 2 * d))
                        nc.scalar.activation(m_sig, m_sig, ACT.Sigmoid).then_inc(m_sig_s, 1)
                        x_square(Place(half + 1), i, d)
                        split_w(here, U_MERGE + 2 * d + 2)
                        act.wait_ge(m_sum, here.nth(d + 1, 2, KT))
                        copy(m_hi[:, i * 2 + d, :], m_f).then_inc(m_hi_s, 1)
                here, after = Place(half), Place(half + 1)
                for k in range(KT):
                    split_h(after, k)
                for u in range(1, 5):
                    split_w(here, U_OUT + u)
                y_square(here, 0)
                y_square(here, 1)
                y_square(here, 2)
                split_w(here, U_OUT + 5)
                split_w(here, U_OUT + 6)
                y_square(here, 3)
                split_w(here, U_OUT + 7)

        @block.gpsimd
        def _(pool):
            count = [0]

            def link(ins, base):
                count[0] += 1
                ins.then_inc(pool_order, 1)
                pool.wait_ge(pool_order, base + count[0])

            def rms(dst, src, base, inv_n, eps):
                count[0] = 0
                link(nc.gpsimd.tensor_tensor(ms[:], src, inv_n[:], ALU.mult), base)
                link(nc.gpsimd.tensor_tensor(ms[:], ms[:], eps[:], ALU.add), base)
                return nc.gpsimd.tensor_tensor(dst, ms[:], minus_half[:], ALU.pow)

            for t, value in ((minus_half, -0.5), (eps_k, EPS), (inv_dm, 1.0 / D_MODEL), (inv_dv, 1.0 / DV)):
                nc.gpsimd.memset(t[:], value).then_inc(pool_order, 1)
            pool.wait_ge(pool_order, 4)
            nc.gpsimd.memset(mean_w[:], 1.0 / D_MODEL).then_inc(mean_ready, 1)
            nc.gpsimd.memset(ones[:], 1.0).then_inc(mean_ready, 1)

            def x_root(here):
                pool.wait_ge(turn_free[0], here.turn_read(0))
                nc.gpsimd.tensor_tensor(x_rs[:], x_ms[:], minus_half[:].to_broadcast([P, TILES]), ALU.pow)\
                    .then_inc(x_rstd, 1)

            nc.gpsimd.memset(state_all[:], 0.0).then_inc(zeroed, 1)
            nc.gpsimd.memset(history[:], 0.0).then_inc(zeroed, 1)
            nc.gpsimd.memset(y_acc[:], 0.0).then_inc(acc_zero, 1)
            pool.wait_ge(consts_in, 16 * CONSTS)
            pool.sem_inc(pool_seen, 1)
            rows, head_part = 2 * TILES, 2 * TILES + 1
            with pool.Fori(0, HALVES) as half:
                here = Place(half)
                order = half * (rows + HEADS * head_part) + 4
                x_root(here)
                with pool.Fori(0, HEADS) as h:
                    nc.gpsimd.tensor_copy(eps_head[:], head_k[:, h, P + 1:P + 2]).then_inc(pool_order, 1)
                    pool.wait_ge(pool_order, order + h * head_part + 1)
                    for t in range(TILES):
                        pool.wait_ge(o_sq, at_head(half, h).nth(t + 1, 4, 16))
                        rms(rstd[:], ssq[:], order + h * head_part + (1 + 2 * t), inv_dv, eps_head).then_inc(o_rstd, 1)
                order = order + HEADS * head_part
                pool.wait_ge(m_sum, here.nth(KT, 0, KT))
                pool.sem_inc(pool_seen, 1)
                nc.gpsimd.memset(y_acc[:], 0.0).then_inc(acc_zero, 1)
                for t in range(TILES):
                    pool.wait_ge(y_sq, here.nth(t + 2, 0, TILES))
                    if t:
                        pool.wait_ge(y_rstd, here.nth(t, 0, TILES))
                    rms(y_rs[:, t:t + 1], y_ssq[:, t:t + 1], order + 2 * t, inv_dm, eps_k).then_inc(y_rstd, 1)

        @block.vector
        def _(dve):
            def rest(dst, src, hi):
                return nc.vector.tensor_tensor(dst, src, hi.bitcast(F32), ALU.subtract)

            def scaled_rest(dst, src, scale, hi):
                return nc.vector.scalar_tensor_tensor(out=dst, in0=src, scalar=scale, in1=hi.bitcast(F32),
                                                      op0=ALU.mult, op1=ALU.subtract)

            def over_rms(here, u, j, dst):
                dve.wait_ge(unit_done, here.used(u))
                nc.vector.tensor_tensor(dst, proj[j % 2][:], x_rs_row[:], ALU.mult).then_inc(proj_free[j % 2], 1)

            def split_w(here, u):
                s = (u + 3) % RING
                dve.wait_ge(w_hi_s, here.split(u + 3))
                rest(w_lo[:, s, :], w_raw[:, s, :], w_hi[:, s, :]).then_inc(w_lo_s, 1)

            def rotate(here, part, j, order, done, n):
                if part == 0:
                    for i in range(2):
                        dve.wait_ge(proj_free[i], here.proj_read(j - 1 + i))
                    dve.wait_ge(rope_done, done)
                else:
                    dve.wait_ge(dve_order, order + 3)
                cos, sin = trig[:, 0, :], trig[:, 1, :]
                first, second, op = ((cos, sin, ALU.subtract), (sin, cos, ALU.add))[part]
                nc.vector.tensor_tensor(pair[:, 0, :], rope_in[:, 0, :], first, ALU.mult).then_inc(dve_order, 1)
                nc.vector.tensor_tensor(pair[:, 1, :], rope_in[:, 1, :], second, ALU.mult).then_inc(dve_order, 1)
                dve.wait_ge(dve_order, order + 3 * part + 2)
                nc.vector.tensor_tensor(kq[:, n + part, :], pair[:, 0, :], pair[:, 1, :], op)\
                    .then_inc(rope_done if part else dve_order, 1)

            def head(half, h, closing):
                here = at_head(half, h)
                for u in range(4):
                    split_w(here, U_HEAD + U_V + u)
                    if u == 1:
                        dve.wait_ge(st_hi_s, here.nth(1, 4, 16))
                        rest(st_lo[:].rearrange("p j e -> p (j e)"), state_all[:, h, :],
                             st_hi[:].rearrange("p j e -> p (j e)")).then_inc(st_lo_s, 1)
                for t in range(TILES):
                    dve.wait_ge(v_hi_s, here.nth(t + 1, 4, 16))
                    scaled_rest(v_lo[:, t, :], wide[t][:], x_rs[:, t:t + 1], v_hi[:, t, :]).then_inc(wide_free[t], 1)
                for t in range(TILES):
                    cols = slice(t * P, (t + 1) * P)
                    dve.wait_ge(turn_full, here.turned(T_HEAD + 2 * t))
                    nc.vector.tensor_tensor(sc_f[:], turn[0][:, 0:P], head_k[:, h, 0:P], ALU.mult)\
                        .then_inc(turn_free[0], 1)
                    dve.wait_ge(q_hi_s, here.nth(t + 1, 4, 16))
                    rest(q_lo[:].rearrange("p (j s) -> p j s", j=2), kq[:, 2:4, cols],
                         q_hi[:].rearrange("p (j s) -> p j s", j=2)).then_inc(q_lo_s, 1)
                    dve.wait_ge(sc_hi_s, here.nth(t + 1, 4, 16))
                    rest(sc_lo[:], sc_f[:], sc_hi[:]).then_inc(sc_lo_s, 1)
                    dve.wait_ge(kn_hi_s, here.nth(t + 1, 4, 16))
                    rest(kn_lo[:], kn_f[:], kn_hi[:]).then_inc(kn_lo_s, 1)
                    split_w(here, U_HEAD + U_G + t)
                    over_rms(here, U_HEAD + U_G + t, J_HEAD + J_G + t, gate[:, t, :])
                    dve.wait_ge(gate_sig, here.nth(t + 1, 4, 16))
                    nc.vector.tensor_tensor(gate[:, t, :], gate[:, t, :], sig[:], ALU.mult).then_inc(gate_done, 1)
                    dve.wait_ge(upd_full, here.nth(t + 1, 4, 16))
                    for j in range(2):
                        kept = state_all[:, h, j * DV:(j + 1) * DV]
                        nc.vector.scalar_tensor_tensor(
                            out=kept if t == TILES - 1 else state[:, j, :], in0=kept if t == 0 else state[:, j, :],
                            scalar=head_k[:, h, P + 2:P + 3], in1=wide[2 + j][:], op0=ALU.mult, op1=ALU.add)\
                            .then_inc(wide_free[2 + j], 1)
                    if t < TILES - 1:
                        dve.wait_ge(st_hi_s, here.nth(t + 2, 4, 16))
                        rest(st_lo[:], state[:], st_hi[:]).then_inc(st_lo_s, 1)

                def gate_o(c):
                    dve.wait_ge(turn_full, here.turned(T_HEAD + T_OT + c))
                    if c == 0:
                        dve.wait_ge(gate_done, here.nth(VT, 4, 16))
                    if c >= 2:
                        dve.wait_ge(yb_lo_s, here.nth(c - 1, 4, 16))
                    nc.vector.tensor_tensor(pair[:, c % 2, :], turn[c % 2][:], gate[:, c, :], ALU.mult)\
                        .then_inc(turn_free[c % 2], 1)

                def split_yb(c):
                    dve.wait_ge(yb_hi_s, here.nth(c + 1, 4, 16))
                    rest(yb_lo[:, c, :], pair[:, c % 2, :], yb_hi[:, c, :]).then_inc(yb_lo_s, 1)

                def filled(i):
                    if closing:
                        over_rms(here, U_HEAD + U_F + i, J_HEAD + J_F + i, kq[:, i, :])

                split_w(here, U_HEAD + U_F)
                filled(0)
                gate_o(0)
                gate_o(1)
                split_yb(0)
                split_yb(1)
                split_w(here, U_HEAD + U_F + 1)
                filled(1)
                gate_o(2)
                gate_o(3)
                split_yb(2)
                split_yb(3)
                order = half * ORDER_HALF + h * 10 + 10
                if not closing:
                    dve.wait_ge(yb_lo_s, here.nth(VT, 4, 16))
                    for part in range(2):
                        rotate(here, part, J_HEAD + J_F + 1, order, here.nth(3, 2, 2 * HEADS), 0)
                for i in (2, 3):
                    split_w(here, U_HEAD + U_F + i)
                    filled(i)
                dve.wait_ge(acc_zero, half + 1)
                for i in range(4):
                    split_w(here, U_HEAD + U_WB + i)
                    for d in range(2):
                        if d:
                            dve.wait_ge(unit_done, here.used(U_HEAD + U_WB + i))
                        else:
                            dve.wait_ge(wb_first, here.nth(i + 1, 4, 16))
                        acc = y_acc[:, 2 * i + d, :]
                        nc.vector.tensor_tensor(acc, acc, proj[d][:], ALU.add).then_inc(proj_free[d], 1)
                        if i < 2 and d == 0 and not closing:
                            rotate(here, i, J_HEAD + J_F + 3, order + 5, here.nth(4, 2, 2 * HEADS), 2)

            for s, n in ((proj_free[0], 1), (proj_free[1], 1), (turn_free[0], 1), (turn_free[1], 1),
                         *((f, 1) for f in wide_free), (rope_done, 1), (pooled, 1)):
                dve.sem_inc(s, n)
            nc.vector.memset(sq_sum[:], 0.0).then_inc(x_sum, 1)

            def add_square(here, i, d):
                dve.wait_ge(x_sq, here.half * KT + 2 * i + (d + 1))
                dve.wait_ge(x_sum, here.half * X_SUMS + 2 * i + (d + 1))
                nc.vector.tensor_tensor(sq_sum[:], sq_sum[:], squares[d][:], ALU.add).then_inc(x_sum, 1)

            def diagonals(here):
                dve.wait_ge(x_rstd, here.nth(1, 0, 1))
                nc.vector.tensor_tensor(x_diag[:],
                                        ident[:].rearrange("p (t s) -> p t s", t=1).to_broadcast([P, TILES, P]),
                                        x_rs[:].rearrange("p (t s) -> p t s", s=1).to_broadcast([P, TILES, P]),
                                        ALU.mult).then_inc(x_diag_s, 1)

            def split_h(here, k):
                dve.wait_ge(h_hi_s, here.nth(k + 1, 0, KT))
                scaled_rest(hT_lo[:, k, :], xT[:, k, :], gain_in[:, k:k + 1], hT_hi[:, k, :]).then_inc(h_lo_s, 1)

            def first_split(u):
                dve.wait_ge(w_hi_s, u + 1)
                rest(w_lo[:, u, :], w_raw[:, u, :], w_hi[:, u, :]).then_inc(w_lo_s, 1)

            for i in range(X_LOADS):
                split_h(Place(0), 2 * i)
                split_h(Place(0), 2 * i + 1)
                if i == 0:
                    first_split(0)
                    first_split(1)
                for d in range(2):
                    add_square(Place(0), i, d)
            first_split(2)
            dve.wait_ge(ident_in, 16)
            dve.wait_ge(zeroed, 2)
            dve.wait_ge(consts_in, 16 * CONSTS)
            with dve.Fori(0, HALVES) as half:
                here = Place(half)
                order = half * ORDER_HALF
                split_w(here, U_KQ)
                diagonals(here)
                split_w(here, U_KQ + 1)
                split_w(here, U_KQ + 2)
                dve.wait_ge(trig_in, half * 16 + 16)
                dve.wait_ge(turn_free[1], here.turn_read(1))
                nc.vector.tensor_tensor(trig[:], trig[:], x_rs_row[:].rearrange("p (c s) -> p c s", c=1)
                                        .to_broadcast([P, 2, TOK]), ALU.mult).then_inc(trig_ready, 1)
                dve.wait_ge(trig_ready, half + 1)
                for i in (1, 3):
                    for part in range(2):
                        rotate(here, part, J_KQ + i, order + i // 2 * 5, here.nth(1 + i // 2, 0, 2 * HEADS), i - 1)
                    if i == 1:
                        split_w(here, U_KQ + 3)
                with dve.Fori(0, HEADS - 1) as h:
                    head(half, h, False)
                head(half, HEADS - 1, True)
                here = Place(half)
                for i in range(2):
                    dve.wait_ge(proj_free[i], here.proj_read(J_POOL - 2 + i))
                dve.wait_ge(gb_sig_s, here.nth(4, 0, 8))
                nc.vector.tensor_tensor(y_acc[:, 0:4, :], y_acc[:, 0:4, :], kq[:], ALU.mult).then_inc(dve_order, 1)

                def take_g_b(here, i):
                    split_w(here, U_GB + i)
                    if i:
                        dve.wait_ge(sig_used, here.nth(i, 0, 4))
                    over_rms(here, U_GB + i, J_GB + i, gb_sig)
                    dve.wait_ge(gb_sig_s, here.nth(5 + i, 0, 8))
                    nc.vector.tensor_tensor(y_acc[:, 4 + i, :], y_acc[:, 4 + i, :], gb_sig, ALU.mult)\
                        .then_inc(sig_used, 1)

                def gate_mixed(here, g, j):
                    dve.wait_ge(turn_full, here.turned(T_MIX + j))
                    dve.wait_ge(a_gate_done, here.nth(j + 1, 2, 2 * GROUPS))
                    nc.vector.scalar_tensor_tensor(
                        out=ya_f[:, j, :], in0=turn[j][:], scalar=scale_k[:, bass.ds(g * 2 + j, 1)],
                        in1=a_gate[:, j, :], op0=ALU.mult, op1=ALU.mult).then_inc(turn_free[j], 1)

                def split_ya(here, g, j):
                    dve.wait_ge(ya_hi_s, here.nth(j + 1, 2, 2 * GROUPS))
                    rest(ya_lo[:, g * 2 + j, :], ya_f[:, j, :], ya_hi[:, g * 2 + j, :]).then_inc(ya_lo_s, 1)

                def pool_group(here, g, ahead):
                    consts = half * GROUPS + g
                    order = half * ORDER_HALF + g * 8 + (ORDER_POOL + 1)
                    past = history[:, g, :].rearrange("p (j s) -> p j s", j=2)
                    split_w(here, U_POOL + 4 * ahead)
                    dve.wait_ge(dve_order, order)
                    dve.wait_ge(pooled, here.nth(1 + ahead, 1, GROUPS))
                    nc.vector.tensor_copy(a_in[:, :, 0:HIST], past).then_inc(dve_order, 1)
                    for j in range(2):
                        over_rms(here, U_POOL + 4 * ahead + j, J_POOL + 4 * ahead + j, a_in[:, j, HIST:])
                        if j == 0:
                            split_w(here, U_POOL + 4 * ahead + 1)
                    for j in range(2):
                        dve.wait_ge(proj_free[j], here.proj_read(J_POOL + 4 * ahead + j))
                    src = a_in
                    for k in range(4):
                        dst = (pa, pb)[k % 2]
                        lo = 2 ** (k + 1) - 1
                        dve.wait_ge(dve_order, order + (k + 1))
                        nc.vector.scalar_tensor_tensor(
                            out=dst[:, :, lo:], in0=src[:, :, lo - 2 ** k:row - 2 ** k],
                            scalar=pool_k[:, consts, k:k + 1], in1=src[:, :, lo:], op0=ALU.mult, op1=ALU.add)\
                            .then_inc(dve_order, 1)
                        src = dst
                        if ahead:
                            if k in (1, 2):
                                gate_mixed(here, g - 1, k - 1)
                            elif k == 3:
                                split_ya(here, g - 1, 0)
                    if ahead:
                        split_ya(here, g - 1, 1)
                    dve.wait_ge(dve_order, order + 5)
                    if ahead:
                        dve.wait_ge(po_lo_s, here.nth(2, 2, 2 * GROUPS))
                    nc.vector.tensor_tensor(
                        tab_tmp[:], src[:, :, HIST:2 * HIST],
                        pool_k[:, bass.ds(consts, 1), 5:5 + HIST].to_broadcast([P, 2, HIST]), ALU.mult)\
                        .then_inc(dve_order, 1)
                    nc.vector.scalar_tensor_tensor(
                        out=po_f[:, :, HIST:], in0=src[:, :, 2 * HIST:], scalar=pool_k[:, consts, 4:5],
                        in1=a_in[:, :, 2 * HIST:], op0=ALU.mult, op1=ALU.subtract).then_inc(dve_order, 1)
                    nc.vector.tensor_copy(past, a_in[:, :, TOK:]).then_inc(dve_order, 1)
                    dve.wait_ge(dve_order, order + 8)
                    nc.vector.tensor_tensor(po_f[:, :, 0:HIST], tab_tmp[:], a_in[:, :, HIST:2 * HIST],
                                            ALU.subtract).then_inc(pooled, 1)

                def group(g, closing):
                    here = at_group(half, g)
                    for i in range(2):
                        over_rms(here, U_POOL + 2 + i, J_POOL + 2 + i, a_gate[:, i, :])
                        split_w(here, U_POOL + 2 + i)
                        dve.wait_ge(a_sig_s, here.nth(i + 1, 2, 2 * GROUPS))
                        nc.vector.tensor_tensor(a_gate[:, i, :], a_gate[:, i, :], a_sig[:, i, :], ALU.mult)\
                            .then_inc(a_gate_done, 1)
                        if i == 0:
                            dve.wait_ge(wp_hi_s, here.nth(1, 1, GROUPS))
                            rest(wp_lo[:], wp_raw[:, g, :], wp_hi[:]).then_inc(wp_lo_s, 1)
                        dve.wait_ge(po_hi_s, here.nth(i + 1, 2, 2 * GROUPS))
                        rest(po_lo[:, i, :], po_f[:, i, :], po_hi[:, i, :]).then_inc(po_lo_s, 1)
                    if closing:
                        for i in range(2):
                            take_g_b(Place(half), i)
                        for j in range(2):
                            gate_mixed(here, g, j)
                        for j in range(2):
                            split_ya(here, g, j)
                    else:
                        pool_group(here, g + 1, 1)

                pool_group(at_group(half, 0), 0, 0)
                with dve.Fori(0, GROUPS - 1) as g:
                    group(g, False)
                group(GROUPS - 1, True)
                for i in (2, 3):
                    take_g_b(here, i)
                split_w(here, U_MERGE)
                dve.wait_ge(ya_lo_s, here.nth(KT, 0, KT))
                nc.vector.memset(sq_sum[:], 0.0).then_inc(x_sum, 1)
                with dve.Fori(0, KT // 2) as i:
                    here = at_merge(half, i)
                    for d in range(2):
                        over_rms(here, U_MERGE + 2 * d, J_MERGE + 2 * d, m_sig)
                        split_w(here, U_MERGE + 2 * d + 1)
                        add_square(Place(half + 1), i, d)
                        if d == 0:
                            dve.wait_ge(sig_used, half * 4 + 4)
                            dve.wait_ge(dve_order, half * ORDER_HALF + ORDER_HALF)
                        dve.wait_ge(m_sig_s, here.nth(d + 1, 2, KT))
                        dve.wait_ge(unit_done, here.used(U_MERGE + 2 * d + 1))
                        nc.vector.tensor_tensor(m_sig, proj[1][:], m_sig, ALU.mult).then_inc(proj_free[1], 1)
                        dve.wait_ge(proj_free[1], here.proj_read(J_MERGE + 2 * d + 1))
                        nc.vector.tensor_tensor(m_f, m_sig, y_acc[:, i * 2 + d, :], ALU.add).then_inc(m_sum, 1)
                        split_w(here, U_MERGE + 2 * d + 2)
                        dve.wait_ge(m_hi_s, here.nth(d + 1, 2, KT))
                        dve.wait_ge(x_sum, (half + 1) * X_SUMS + 2 * i + (d + 2))
                        rest(m_lo[:, i * 2 + d, :], m_f, m_hi[:, i * 2 + d, :]).then_inc(m_lo_s, 1)
                        dve.wait_ge(m_lo_s, here.nth(d + 1, 2, KT))
                here, after = Place(half), Place(half + 1)

                def residual(e, t):
                    if t < TILES - 1:
                        dve.wait_ge(out_full, here.nth(e * (TILES - 1) + t + 1, 0, 2 * (TILES - 1)))
                    else:
                        dve.wait_ge(unit_done, here.used(U_OUT + 4 * e + 3))
                    cols = slice(e * 512, (e + 1) * 512)
                    nc.vector.tensor_tensor(y[:, t, cols], y[:, t, cols], wide[t][:], ALU.add).then_inc(wide_free[t], 1)

                def normalise(t, pieces=1):
                    dve.wait_ge(y_rstd, here.nth(t + 1, 0, TILES))
                    for i in range(pieces):
                        cols = slice(i * D_MODEL // pieces, (i + 1) * D_MODEL // pieces)
                        nc.vector.scalar_tensor_tensor(
                            out=y[:, t, cols], in0=y[:, t, cols], scalar=y_rs[:, t:t + 1], in1=gain_out[:, cols],
                            op0=ALU.mult, op1=ALU.mult).then_inc(y_ready, 1)

                for k in range(KT):
                    split_h(after, k)
                dve.wait_ge(y_in, half * (16 * (TILES + 1)) + 16 * (TILES + 1))
                for t in range(TILES - 1):
                    residual(0, t)
                for u in range(1, 4):
                    split_w(here, U_OUT + u)
                residual(0, 3)
                split_w(here, U_OUT + 4)
                residual(1, 0)
                residual(1, 1)
                normalise(0)
                residual(1, 2)
                normalise(1)
                split_w(here, U_OUT + 5)
                split_w(here, U_OUT + 6)
                residual(1, 3)
                normalise(2)
                split_w(here, U_OUT + 7)
                normalise(3, 2)


def weight_units(w_in, w_a, w_b, w_o):
    offs = np.cumsum((0, 1024, 1024, 1024, 1024, 2048, 2048, 1024, 1024))
    a_in, a_gate, q, k, v, r_gate, g_a, g_b = (w_in[:, offs[i]:offs[i + 1]] for i in range(8))

    def tiles(w, k, e, cols=P):
        rows = w[k[0] * P:k[1] * P, e:e + cols]
        return rows.reshape(k[1] - k[0], P, cols).transpose(1, 0, 2).reshape(P, -1)

    def kq_units(h):
        return [tiles(w, (0, KT), h * DK + j * P) for w in (k, q) for j in range(2)]

    units = kq_units(0)
    for h in range(HEADS):
        units += [tiles(v, (2 * u, 2 * u + 2), h * DV, DV) for u in range(4)]
        units += [tiles(r_gate, (0, KT), h * DV + c * P) for c in range(VT)]
        units += kq_units(h + 1) if h < HEADS - 1 else [tiles(g_b, (0, KT), i * P) for i in range(4)]
        units += [tiles(w_b, (h * VT, (h + 1) * VT), i * 2 * P, 2 * P) for i in range(4)]
    for g in range(GROUPS):
        units += [tiles(w, (0, KT), g * GROUP + j * P) for w in (a_in, a_gate) for j in range(2)]
    units += [tiles(g_b, (0, KT), (4 + i) * P) for i in range(4)]
    for d in range(KT):
        units += [tiles(g_a, (0, KT), d * P), tiles(w_a, (0, KT), d * P)]
    for e in range(2):
        units += [tiles(w_o, (2 * u, 2 * u + 2), e * 512, 512) for u in range(4)]
    assert len(units) == UNITS
    return np.ascontiguousarray(np.stack(units))


def shape_constants():
    half = DK // 2
    inv_freq = (1.0 / (np.float32(ROPE_BASE) ** (np.arange(half, dtype=np.float32) / np.float32(half)))).astype(np.float32)
    angle = np.arange(SEQ, dtype=np.float32)[None, :] * inv_freq[:, None]
    trig = np.stack([np.cos(angle.astype(np.float64)), np.sin(angle.astype(np.float64))], 1)
    trig = trig.reshape(P, 2, HALVES, TOK).transpose(2, 0, 1, 3)

    head = np.zeros((P, HEADS, HC))
    i = np.arange(P)
    for h in range(HEADS):
        gamma = 1.0 - 2.0 ** (-5.0 - h)
        seen = (i[:, None] // CHUNK) <= (i[None, :] // CHUNK)
        head[:, h, 0:P] = seen * gamma ** (np.abs(i[:, None] - i[None, :]) - (i[None, :] + 1.0)) * DK ** -0.5
        head[:, h, P] = gamma ** (P - 1.0 - i) * DK ** -0.5
        head[:, h, P + 1] = EPS / gamma ** (2.0 * (i + 1))
        head[:, h, P + 2] = gamma ** P

    pool = np.zeros((HALVES, GROUPS, PCOLS))
    for s in range(HALVES):
        for g, w in enumerate(WINDOWS):
            pool[s, g, 0:4] = [2 ** k < w for k in range(4)]
            pool[s, g, 4] = 1.0 / w
            pool[s, g, 5:] = 1.0 / np.minimum(s * TOK + np.arange(HIST) + 1, w)
    pool = np.broadcast_to(pool.reshape(1, HALVES * GROUPS, PCOLS), (P, HALVES * GROUPS, PCOLS))
    return [np.ascontiguousarray(a.astype(np.float32)) for a in (np.eye(P), trig, head, pool)]


def kernel(**inputs):
    import concourse.bacc as bacc
    from concourse.bass_utils import run_bass_kernel_spmd

    a = {n: np.asarray(v) for n, v in inputs.items()}
    ident, trig, head, pool = shape_constants()
    arrays = {
        "wstream": weight_units(a["w_in"], a["w_a"], a["w_b"], a["w_o"]),
        "x": a["x"],
        "x_turned": np.ascontiguousarray(a["x"].reshape(HALVES, TOK, KT, P).transpose(0, 3, 2, 1)
                                         .reshape(HALVES, P, KT * TOK)),
        "norm_in": np.ascontiguousarray(a["norm_in"].reshape(KT, P).T),
        "w_pool": np.ascontiguousarray(a["w_pool"].reshape(GROUPS, 2, P, GROUP).transpose(2, 0, 1, 3)
                                       .reshape(P, GROUPS, 2 * GROUP)),
        "pool_scale": np.ascontiguousarray(a["pool_scale"].reshape(KT, P).T),
        "norm_out": np.ascontiguousarray(np.broadcast_to(a["norm_out"], (P, D_MODEL))),
        "ident": ident, "trig": trig, "head": head, "pool": pool,
    }
    nc = bacc.Bacc("TRN2", target_bir_lowering=False, num_devices=1)
    args = [nc.dram_tensor(f"in_{n}", v.shape, F32, kind="ExternalInput").ap() for n, v in arrays.items()]
    out = nc.dram_tensor("out", (1, SEQ, D_MODEL), F32, kind="ExternalOutput").ap()
    build(nc, *args, out)
    r = run_bass_kernel_spmd(nc, [{f"in_{n}": v for n, v in arrays.items()}], core_ids=[0])
    return r.results[0]["out"]
```
